# Optimizing a Trainium2 kernel written in Bass

```python
import numpy as np
import jax
import jax.numpy as jnp
from jax import lax
import math
import jax, jax.numpy as jnp

D_MODEL = 2048
BATCH = 1
SEQ = 256
DEPTH = 1

CHUNK = 64
N_MEM = 256
NORM_EPS = 1e-6
NEG_INF = -1e30

A_HEADS = 8
A_HEAD_DIM = 128
A_WIDTH = A_HEADS * A_HEAD_DIM
A_LEFT_CHUNKS = 8
A_BAND = (A_LEFT_CHUNKS + 1) * CHUNK
REL_CLIP = 128

B_HEADS = 16
B_HEAD_DIM = 64
B_WIDTH = B_HEADS * B_HEAD_DIM
DECAY_LORA = 64
ICLR_LORA = 64
GN_EPS = 64e-5

C_HEADS = 4
C_HEAD_DIM = 256
C_WIDTH = C_HEADS * C_HEAD_DIM

IN_SPLITS = (A_WIDTH,) * 4 + (B_WIDTH,) * 4 + (DECAY_LORA, ICLR_LORA) + (C_WIDTH,) * 2 + (D_MODEL,) * 3
IN_COLS = sum(IN_SPLITS)


def rms_norm(x, g):
    xf = x.astype(jnp.float32)
    y = xf * lax.rsqrt(jnp.mean(xf * xf, axis=-1, keepdims=True) + NORM_EPS)
    return (y * g.astype(jnp.float32)).astype(x.dtype)

def _rel_index():
    r = np.arange(CHUNK)[:, None]
    m = np.arange(A_BAND)[None, :]
    dist = r + A_LEFT_CHUNKS * CHUNK - m
    return np.clip(dist, -REL_CLIP, REL_CLIP) + REL_CLIP

def chunked_band_attention(q, k, v, rel_bias):
    bsz, s, h, dh = q.shape
    n_chunks = s // CHUNK
    pad = A_LEFT_CHUNKS * CHUNK
    kp = jnp.pad(k, ((0, 0), (pad, 0), (0, 0), (0, 0)))
    vp = jnp.pad(v, ((0, 0), (pad, 0), (0, 0), (0, 0)))
    bias = rel_bias[:, _rel_index()].astype(jnp.float32)
    band_pos = jnp.arange(A_BAND) - pad
    scale = dh ** -0.5

    def one_chunk(c):
        start = c * CHUNK
        qc = lax.dynamic_slice_in_dim(q, start, CHUNK, axis=1)
        kc = lax.dynamic_slice_in_dim(kp, start, A_BAND, axis=1)
        vc = lax.dynamic_slice_in_dim(vp, start, A_BAND, axis=1)
        sc = jnp.einsum('bqhd,bkhd->bhqk', qc, kc, preferred_element_type=jnp.float32) * scale + bias
        valid = (start + band_pos) >= 0
        sc = jnp.where(valid[None, None, None, :], sc, NEG_INF)
        p = jax.nn.softmax(sc, axis=-1)
        return jnp.einsum('bhqk,bkhd->bqhd', p.astype(vc.dtype), vc)

    out = lax.map(one_chunk, jnp.arange(n_chunks))
    return jnp.transpose(out, (1, 0, 2, 3, 4)).reshape(bsz, s, h * dh)

def token_shift_lerp(p, mu):
    prev = jnp.pad(p, ((0, 0), (1, 0), (0, 0)))[:, :-1]
    return p + mu * (prev - p)

def rwkv7_scan(r, decay, k, v, a_vec, b_vec):
    bsz, _, h, n = r.shape

    def step(state, inp):
        r_t, w_t, k_t, v_t, a_t, b_t = inp
        sa = jnp.einsum('bhij,bhj->bhi', state, a_t)
        state = state * w_t[:, :, None, :] + sa[..., None] * b_t[:, :, None, :] + v_t[..., None] * k_t[:, :, None, :]
        return state, jnp.einsum('bhij,bhj->bhi', state, r_t)

    xs = tuple(jnp.moveaxis(t, 1, 0) for t in (r, decay, k, v, a_vec, b_vec))
    s0 = jnp.zeros((bsz, h, n, n), jnp.float32)
    _, out = lax.scan(step, s0, xs)
    return jnp.moveaxis(out, 0, 1)

def rwkv7_time_mix(p_r, p_k, p_v, p_wd, p_ad, mu_rkv, mu_w, mu_a, w0, w2, a0, a2, k_k, k_a, r_k, ln_w, ln_b):
    f = lambda t: t.astype(jnp.float32)
    p_r, p_k, p_v, p_wd, p_ad = f(p_r), f(p_k), f(p_v), f(p_wd), f(p_ad)
    bsz, s, _ = p_r.shape
    r = token_shift_lerp(p_r, f(mu_rkv[0]))
    k = token_shift_lerp(p_k, f(mu_rkv[1]))
    v = token_shift_lerp(p_v, f(mu_rkv[2]))
    wd = token_shift_lerp(p_wd, f(mu_w))
    ad = token_shift_lerp(p_ad, f(mu_a))
    w = -jax.nn.softplus(-(f(w0) + jnp.tanh(wd) @ f(w2))) - 0.5
    decay = jnp.exp(-jnp.exp(w))
    a = jax.nn.sigmoid(f(a0) + ad @ f(a2))
    heads = lambda t: t.reshape(bsz, s, B_HEADS, B_HEAD_DIM)
    kk = heads(k * f(k_k))
    kk = kk * lax.rsqrt(jnp.maximum(jnp.sum(kk * kk, axis=-1, keepdims=True), 1e-24))
    k = k * (1.0 + (a - 1.0) * f(k_a))
    rh, kh, vh, ah, dh = heads(r), heads(k), heads(v), heads(a), heads(decay)
    o = rwkv7_scan(rh, dh, kh, vh, -kk, kk * ah)
    mean = jnp.mean(o, axis=-1, keepdims=True)
    var = jnp.mean(jnp.square(o - mean), axis=-1, keepdims=True)
    o = ((o - mean) * lax.rsqrt(var + GN_EPS)).reshape(bsz, s, B_WIDTH) * f(ln_w) + f(ln_b)
    bonus = jnp.sum(rh * kh * f(r_k), axis=-1, keepdims=True) * vh
    return o + bonus.reshape(bsz, s, B_WIDTH)

def memory_cross_attention(q, mk, mv):
    bsz, s, h, dh = q.shape
    sc = jnp.einsum('bshd,bmhd->bhsm', q, mk, preferred_element_type=jnp.float32) * (dh ** -0.5)
    p = jax.nn.softmax(sc, axis=-1)
    out = jnp.einsum('bhsm,bmhd->bshd', p.astype(mv.dtype), mv)
    return out.reshape(bsz, s, h * dh)

def hybrid_layer(x, mem, norm_g, w_in, a_q_g, a_k_g, a_rel_bias, w_up_a,
                 b_mu_rkv, b_mu_w, b_mu_a, b_w0, b_w2, b_a0, b_a2, b_k_k, b_k_a, b_r_k,
                 b_ln_w, b_ln_b, w_up_b, mem_norm_g, w_mem_kv, c_q_g, c_k_g, w_up_c, w_o):
    bsz, s, _ = x.shape
    h = rms_norm(x, norm_g)
    proj = h @ w_in
    offsets = np.cumsum(np.array(IN_SPLITS))[:-1].tolist()
    (aq, ak, av, az, br, bk, bv, bz, bwd, bad, cq, cz, ga, gb, gc) = jnp.split(proj, offsets, axis=-1)

    aq = rms_norm(aq.reshape(bsz, s, A_HEADS, A_HEAD_DIM), a_q_g)
    ak = rms_norm(ak.reshape(bsz, s, A_HEADS, A_HEAD_DIM), a_k_g)
    av = av.reshape(bsz, s, A_HEADS, A_HEAD_DIM)
    ya = chunked_band_attention(aq, ak, av, a_rel_bias) * jax.nn.silu(az)

    yb = rwkv7_time_mix(br, bk, bv, bwd, bad, b_mu_rkv, b_mu_w, b_mu_a, b_w0, b_w2, b_a0, b_a2,
                        b_k_k, b_k_a, b_r_k, b_ln_w, b_ln_b).astype(x.dtype) * jax.nn.silu(bz)

    m = rms_norm(mem, mem_norm_g)
    mk, mv = jnp.split(m @ w_mem_kv, 2, axis=-1)
    mk = rms_norm(mk.reshape(bsz, N_MEM, C_HEADS, C_HEAD_DIM), c_k_g)
    mv = mv.reshape(bsz, N_MEM, C_HEADS, C_HEAD_DIM)
    cq = rms_norm(cq.reshape(bsz, s, C_HEADS, C_HEAD_DIM), c_q_g)
    yc = memory_cross_attention(cq, mk, mv) * jax.nn.silu(cz)

    merged = (jax.nn.sigmoid(ga) * (ya @ w_up_a)
              + jax.nn.sigmoid(gb) * (yb @ w_up_b)
              + jax.nn.sigmoid(gc) * (yc @ w_up_c))
    return x + merged @ w_o

def first_inputs(seed: int = 0) -> dict:
    key = jax.random.key(seed)
    ks = jax.random.split(key, 32)
    nrm = lambda k, shape, sc: jax.random.normal(k, shape, jnp.float32) * sc
    L = DEPTH
    return {
        "x": nrm(ks[0], (BATCH, SEQ, D_MODEL), 1.0),
        "mem": nrm(ks[1], (BATCH, N_MEM, D_MODEL), 1.0),
        "norm_g": 1.0 + nrm(ks[2], (L, D_MODEL), 0.1),
        "w_in": nrm(ks[3], (L, D_MODEL, IN_COLS), D_MODEL ** -0.5),
        "a_q_g": 1.0 + nrm(ks[4], (L, A_HEAD_DIM), 0.1),
        "a_k_g": 1.0 + nrm(ks[5], (L, A_HEAD_DIM), 0.1),
        "a_rel_bias": nrm(ks[6], (L, A_HEADS, 2 * REL_CLIP + 1), 0.5),
        "w_up_a": nrm(ks[7], (L, A_WIDTH, D_MODEL), A_WIDTH ** -0.5),
        "b_mu_rkv": jax.random.uniform(ks[8], (L, 3, B_WIDTH), jnp.float32),
        "b_mu_w": jax.random.uniform(ks[9], (L, DECAY_LORA), jnp.float32),
        "b_mu_a": jax.random.uniform(ks[10], (L, ICLR_LORA), jnp.float32),
        "b_w0": jax.random.uniform(ks[11], (L, B_WIDTH), jnp.float32, minval=-3.0, maxval=0.5),
        "b_w2": nrm(ks[12], (L, DECAY_LORA, B_WIDTH), 0.1),
        "b_a0": nrm(ks[13], (L, B_WIDTH), 0.5),
        "b_a2": nrm(ks[14], (L, ICLR_LORA, B_WIDTH), 0.1),
        "b_k_k": 0.85 + nrm(ks[15], (L, B_WIDTH), 0.05),
        "b_k_a": 1.0 + nrm(ks[16], (L, B_WIDTH), 0.05),
        "b_r_k": nrm(ks[17], (L, B_HEADS, B_HEAD_DIM), 0.1),
        "b_ln_w": 1.0 + nrm(ks[18], (L, B_WIDTH), 0.1),
        "b_ln_b": nrm(ks[19], (L, B_WIDTH), 0.02),
        "w_up_b": nrm(ks[20], (L, B_WIDTH, D_MODEL), B_WIDTH ** -0.5),
        "mem_norm_g": 1.0 + nrm(ks[21], (L, D_MODEL), 0.1),
        "w_mem_kv": nrm(ks[22], (L, D_MODEL, 2 * C_WIDTH), D_MODEL ** -0.5),
        "c_q_g": 1.0 + nrm(ks[23], (L, C_HEAD_DIM), 0.1),
        "c_k_g": 1.0 + nrm(ks[24], (L, C_HEAD_DIM), 0.1),
        "w_up_c": nrm(ks[25], (L, C_WIDTH, D_MODEL), C_WIDTH ** -0.5),
        "w_o": nrm(ks[26], (L, D_MODEL, D_MODEL), D_MODEL ** -0.5),
    }

def first_block(x, mem, norm_g, w_in, a_q_g, a_k_g, a_rel_bias, w_up_a,
              b_mu_rkv, b_mu_w, b_mu_a, b_w0, b_w2, b_a0, b_a2, b_k_k, b_k_a, b_r_k,
              b_ln_w, b_ln_b, w_up_b, mem_norm_g, w_mem_kv, c_q_g, c_k_g, w_up_c, w_o):
    for l in range(DEPTH):
        x = hybrid_layer(x, mem, norm_g[l], w_in[l], a_q_g[l], a_k_g[l], a_rel_bias[l], w_up_a[l],
                         b_mu_rkv[l], b_mu_w[l], b_mu_a[l], b_w0[l], b_w2[l], b_a0[l], b_a2[l],
                         b_k_k[l], b_k_a[l], b_r_k[l], b_ln_w[l], b_ln_b[l], w_up_b[l],
                         mem_norm_g[l], w_mem_kv[l], c_q_g[l], c_k_g[l], w_up_c[l], w_o[l])
    return x


BRANCH_WIDTH = D_MODEL // 2
N_BRANCH = 3
ATTN_HEAD_DIM = 128
ATTN_HEADS = BRANCH_WIDTH // ATTN_HEAD_DIM
ATTN_WIDTH = ATTN_HEADS * ATTN_HEAD_DIM
MOBA_BLOCK = 256
MOBA_TOPK = 3
QUERY_CHUNK = 64
GLA_HEADS = 4
GLA_VAL_DIM = BRANCH_WIDTH // GLA_HEADS
GLA_KEY_DIM = GLA_VAL_DIM // 2
GLA_KEY_WIDTH = GLA_HEADS * GLA_KEY_DIM
GLA_VAL_WIDTH = GLA_HEADS * GLA_VAL_DIM
GLA_GATE_RANK = 16
GLA_GATE_TAU = 16.0
GLA_CHUNK = 64
CONV_WIDTH = BRANCH_WIDTH
CONV_K = 3
D_FF = -(-8 * D_MODEL // (3 * 256)) * 256
RMS_EPS = 1e-6
COL_SIZES = (ATTN_WIDTH, ATTN_WIDTH, ATTN_WIDTH,
             GLA_KEY_WIDTH, GLA_KEY_WIDTH, GLA_VAL_WIDTH,
             GLA_VAL_WIDTH, GLA_GATE_RANK,
             CONV_WIDTH, CONV_WIDTH, CONV_WIDTH,
             N_BRANCH * D_MODEL)
N_IN_COLS = sum(COL_SIZES)


def rms_norm_2(x, w):
    xf = x.astype(jnp.float32)
    y = xf * lax.rsqrt(jnp.mean(xf * xf, axis=-1, keepdims=True) + RMS_EPS)
    return (y * w.astype(jnp.float32)).astype(x.dtype)

def moba_attention(q, k, v):
    B_, S, H, dh = q.shape
    f32 = jnp.float32
    nb = -(-S // MOBA_BLOCK)
    s_pad = nb * MOBA_BLOCK
    topk = min(MOBA_TOPK, nb)
    pad = ((0, 0), (0, s_pad - S), (0, 0), (0, 0))
    kp = jnp.pad(k, pad)
    vp = jnp.pad(v, pad)
    kb = kp.reshape(B_, nb, MOBA_BLOCK, H, dh).transpose(0, 3, 1, 2, 4)
    vb = vp.reshape(B_, nb, MOBA_BLOCK, H, dh).transpose(0, 3, 1, 2, 4)
    k_mean = jnp.mean(kb.astype(f32), axis=3)
    slopes = 2.0 ** (-8.0 * jnp.arange(1, H + 1, dtype=f32) / H)
    scale = 1.0 / math.sqrt(dh)
    bi = jnp.arange(B_)[:, None, None, None]
    hi = jnp.arange(H)[None, None, :, None]
    blk_ids = jnp.arange(nb)
    in_blk = jnp.arange(MOBA_BLOCK)

    def one_chunk(c):
        start = c * QUERY_CHUNK
        qf = lax.dynamic_slice_in_dim(q, start, QUERY_CHUNK, axis=1).astype(f32)
        t_pos = start + jnp.arange(QUERY_CHUNK)
        own = start // MOBA_BLOCK
        gate = jnp.einsum("bqhd,bhnd->bqhn", qf, k_mean)
        gate = jnp.where((blk_ids < own)[None, None, None, :], gate, -jnp.inf)
        _, sel = lax.top_k(gate, topk)
        sel_valid = sel < own
        k_sel = kb[bi, hi, sel].astype(f32)
        v_sel = vb[bi, hi, sel].astype(f32)
        s_sel = jnp.einsum("bqhd,bqhnkd->bqhnk", qf, k_sel) * scale
        kpos_sel = sel[..., None] * MOBA_BLOCK + in_blk
        dist_sel = (t_pos[None, :, None, None, None] - kpos_sel).astype(f32)
        s_sel = s_sel - slopes[None, None, :, None, None] * dist_sel
        s_sel = jnp.where(sel_valid[..., None], s_sel, -jnp.inf)
        k_own = lax.dynamic_slice_in_dim(kp, own * MOBA_BLOCK, MOBA_BLOCK, axis=1).astype(f32)
        v_own = lax.dynamic_slice_in_dim(vp, own * MOBA_BLOCK, MOBA_BLOCK, axis=1).astype(f32)
        s_own = jnp.einsum("bqhd,bkhd->bqhk", qf, k_own) * scale
        dist_own = t_pos[:, None] - (own * MOBA_BLOCK + in_blk)[None, :]
        s_own = s_own - slopes[None, None, :, None] * dist_own[None, :, None, :].astype(f32)
        s_own = jnp.where((dist_own >= 0)[None, :, None, :], s_own, -jnp.inf)
        n_sel = topk * MOBA_BLOCK
        p = jax.nn.softmax(jnp.concatenate(
            [s_sel.reshape(B_, QUERY_CHUNK, H, n_sel), s_own], axis=-1), axis=-1)
        p_sel = p[..., :n_sel].reshape(B_, QUERY_CHUNK, H, topk, MOBA_BLOCK)
        out = (jnp.einsum("bqhnk,bqhnkd->bqhd", p_sel, v_sel)
               + jnp.einsum("bqhk,bkhd->bqhd", p[..., n_sel:], v_own))
        return out.astype(q.dtype)

    outs = lax.map(one_chunk, jnp.arange(S // QUERY_CHUNK))
    return outs.transpose(1, 0, 2, 3, 4).reshape(B_, S, H, dh)

def gla_attention(q, k, v, log_a):
    B_, S, H, dk = q.shape
    dv = v.shape[-1]
    f32 = jnp.float32
    n = S // GLA_CHUNK

    def chunked(t):
        return t.astype(f32).reshape(B_, n, GLA_CHUNK, H, t.shape[-1]).transpose(0, 3, 1, 2, 4)

    qc = chunked(q) * (dk ** -0.5)
    kc, vc = chunked(k), chunked(v)
    b = jnp.cumsum(chunked(log_a), axis=3)
    b_last = b[..., -1:, :]
    q_in = qc * jnp.exp(b)
    k_in = kc * jnp.exp(-b)
    k_dec = kc * jnp.exp(b_last - b)
    causal = jnp.tril(jnp.ones((GLA_CHUNK, GLA_CHUNK), dtype=bool))
    a_intra = jnp.where(causal, jnp.einsum("bhncd,bhnsd->bhncs", q_in, k_in), 0.0)
    o_intra = jnp.einsum("bhncs,bhnse->bhnce", a_intra, vc)
    kv = jnp.einsum("bhncd,bhnce->bhnde", k_dec, vc)
    decay = jnp.exp(b_last[..., 0, :])

    def step(state, inp):
        kv_n, d_n = inp
        return d_n[..., None] * state + kv_n, state

    _, s_prev = lax.scan(step, jnp.zeros((B_, H, dk, dv), f32),
                         (kv.transpose(2, 0, 1, 3, 4), decay.transpose(2, 0, 1, 3)))
    s_prev = s_prev.transpose(1, 2, 0, 3, 4)
    o = o_intra + jnp.einsum("bhncd,bhnde->bhnce", q_in, s_prev)
    return o.transpose(0, 2, 3, 1, 4).reshape(B_, S, H, dv)

def short_conv(u, w):
    ch = u.shape[-1]
    return lax.conv_general_dilated(
        u, w[:, None, :].astype(u.dtype), window_strides=(1,), padding=[(CONV_K - 1, 0)],
        dimension_numbers=("NWC", "WIO", "NWC"), feature_group_count=ch)

def second_inputs(seed: int = 0) -> dict:
    key = jax.random.key(seed)
    ks = jax.random.split(key, 16)
    L, D = DEPTH, D_MODEL
    nrm = lambda k, shape, s: jax.random.normal(k, shape, jnp.float32) * s
    gain = lambda k, shape: 1.0 + 0.02 * jax.random.normal(k, shape, jnp.float32)
    return {
        "x": nrm(ks[0], (BATCH, SEQ, D), 1.0),
        "norm1_w": gain(ks[1], (L, D)),
        "w_in": nrm(ks[2], (L, D, N_IN_COLS), D ** -0.5),
        "gla_w_up": nrm(ks[3], (L, GLA_GATE_RANK, GLA_KEY_WIDTH), GLA_GATE_RANK ** -0.5),
        "gla_b": nrm(ks[4], (L, GLA_KEY_WIDTH), 0.02),
        "gla_norm_w": gain(ks[5], (L, GLA_VAL_DIM)),
        "conv_w": nrm(ks[6], (L, CONV_K, CONV_WIDTH), CONV_K ** -0.5),
        "w_br_attn": nrm(ks[7], (L, ATTN_WIDTH, D), ATTN_WIDTH ** -0.5),
        "w_br_gla": nrm(ks[8], (L, GLA_VAL_WIDTH, D), GLA_VAL_WIDTH ** -0.5),
        "w_br_conv": nrm(ks[9], (L, CONV_WIDTH, D), CONV_WIDTH ** -0.5),
        "w_out": nrm(ks[10], (L, D, D), D ** -0.5),
        "norm2_w": gain(ks[11], (L, D)),
        "w_ffn_gate": nrm(ks[12], (L, D, D_FF), D ** -0.5),
        "w_ffn_up": nrm(ks[13], (L, D, D_FF), D ** -0.5),
        "w_ffn_down": nrm(ks[14], (L, D_FF, D), D_FF ** -0.5),
        "final_norm_w": gain(ks[15], (D,)),
    }

def second_block(x, norm1_w, w_in, gla_w_up, gla_b, gla_norm_w, conv_w, w_br_attn, w_br_gla,
              w_br_conv, w_out, norm2_w, w_ffn_gate, w_ffn_up, w_ffn_down, final_norm_w):
    B_, S, D = x.shape
    f32 = jnp.float32
    splits = [int(s) for s in np.cumsum(COL_SIZES)[:-1]]
    for l in range(DEPTH):
        h = rms_norm_2(x, norm1_w[l])
        proj = h @ w_in[l]
        (q_a, k_a, v_a, q_g, k_g, v_g, r_g, a_down,
         b_gate, c_gate, u_conv, merge) = jnp.split(proj, splits, axis=-1)
        hs_a = (B_, S, ATTN_HEADS, ATTN_HEAD_DIM)
        o_a = moba_attention(q_a.reshape(hs_a), k_a.reshape(hs_a), v_a.reshape(hs_a))
        br_a = o_a.reshape(B_, S, ATTN_WIDTH) @ w_br_attn[l]
        z = (a_down @ gla_w_up[l]).astype(f32) + gla_b[l].astype(f32)
        log_a = jax.nn.log_sigmoid(z) / GLA_GATE_TAU
        hs_k = (B_, S, GLA_HEADS, GLA_KEY_DIM)
        o_g = gla_attention(q_g.reshape(hs_k), k_g.reshape(hs_k),
                            v_g.reshape(B_, S, GLA_HEADS, GLA_VAL_DIM), log_a.reshape(hs_k))
        o_g = o_g * lax.rsqrt(jnp.mean(o_g * o_g, axis=-1, keepdims=True) + RMS_EPS)
        o_g = o_g * gla_norm_w[l].astype(f32)
        o_g = o_g.reshape(B_, S, GLA_VAL_WIDTH) * jax.nn.silu(r_g.astype(f32))
        br_b = o_g.astype(x.dtype) @ w_br_gla[l]
        y_c = b_gate * short_conv(c_gate * u_conv, conv_w[l])
        br_c = y_c @ w_br_conv[l]
        g = jax.nn.sigmoid(merge.astype(f32)).reshape(B_, S, N_BRANCH, D)
        mixed = (g[:, :, 0] * br_a.astype(f32) + g[:, :, 1] * br_b.astype(f32)
                 + g[:, :, 2] * br_c.astype(f32)).astype(x.dtype)
        x = x + mixed @ w_out[l]
        h2 = rms_norm_2(x, norm2_w[l])
        x = x + (jax.nn.silu(h2 @ w_ffn_gate[l]) * (h2 @ w_ffn_up[l])) @ w_ffn_down[l]
    return rms_norm_2(x, final_norm_w)


def setup_inputs(seed=0):
    out = dict(first_inputs(seed))
    for name, value in second_inputs(seed + 1).items():
        if name != "x":
            out[name + "_2"] = value
    return out


def reference(
    x, mem, norm_g, w_in, a_q_g, a_k_g, a_rel_bias, w_up_a, b_mu_rkv, b_mu_w, b_mu_a, b_w0,
    b_w2, b_a0, b_a2, b_k_k, b_k_a, b_r_k, b_ln_w, b_ln_b, w_up_b, mem_norm_g, w_mem_kv, c_q_g,
    c_k_g, w_up_c, w_o, norm1_w_2, w_in_2, gla_w_up_2, gla_b_2, gla_norm_w_2, conv_w_2,
    w_br_attn_2, w_br_gla_2, w_br_conv_2, w_out_2, norm2_w_2, w_ffn_gate_2, w_ffn_up_2,
    w_ffn_down_2, final_norm_w_2,
):
    x = first_block(
        x, mem, norm_g, w_in, a_q_g, a_k_g, a_rel_bias, w_up_a, b_mu_rkv, b_mu_w, b_mu_a, b_w0,
        b_w2, b_a0, b_a2, b_k_k, b_k_a, b_r_k, b_ln_w, b_ln_b, w_up_b, mem_norm_g, w_mem_kv,
        c_q_g, c_k_g, w_up_c, w_o,
    )
    return second_block(
        x, norm1_w_2, w_in_2, gla_w_up_2, gla_b_2, gla_norm_w_2, conv_w_2, w_br_attn_2,
        w_br_gla_2, w_br_conv_2, w_out_2, norm2_w_2, w_ffn_gate_2, w_ffn_up_2, w_ffn_down_2,
        final_norm_w_2,
    )


_drawn_inputs = setup_inputs


def setup_inputs(seed=0):
    import zlib

    import numpy as np

    out = dict(_drawn_inputs(seed))
    spreads = {}
    factors = {'a_q_g': 8.0,
     'a_k_g': 7.344,
     'b_mu_w': 29.662,
     'b_k_k': 62.408,
     'b_ln_b': 6.51,
     'mem_norm_g': 8.0,
     'c_q_g': 8.0,
     'c_k_g': 8.0,
     'gla_b_2': 8.0,
     'gla_norm_w_2': 23.996,
     'norm2_w_2': 4.585,
     'final_norm_w_2': 8.481,
     'a_rel_bias': 3.554,
     'b_k_a': 3.817}
    for name, (base, spread) in spreads.items():
        noise = np.random.default_rng([zlib.crc32(name.encode()), seed]).standard_normal(out[name].shape)
        drawn = base * np.exp(spread * noise) if base else spread * noise
        out[name] = jnp.asarray(drawn.astype(out[name].dtype))
    for name, factor in factors.items():
        out[name] = (out[name] * factor).astype(out[name].dtype)
    return out
```

```python
from collections import Counter, namedtuple
from contextlib import ExitStack

import numpy as np

import concourse.bass as bass
from concourse import mybir

ALU = mybir.AluOpType
ACT = mybir.ActivationFunctionType
F32 = mybir.dt.float32
F32R = mybir.dt.float32r
U8 = mybir.dt.uint8
AX = mybir.AxisListType.X

P = 128
T = 256
D = 2048
KD = D // P
BW = 1024
KB = BW // P
CHUNK = 128
FF = 5632
KF = FF // P
UNIT = 1024
RING = 4
LEAD = 3
EPS = 1e-6
GN_EPS = 64e-5
KAPPA = float(np.exp(-0.5))
MASKED = -1e30
LEVELS = 7

A_COL, B_COL, LORA_COL, C_COL = 0, 4096, 8192, 8320
GA_COL, GB_COL, GC_COL = 10368, 12416, 14464
Q_COL, L_COL, DOWN_COL, V_COL, M_COL = 0, 3072, 6144, 6160, 9232

Block = namedtuple("Block", "weight kt kind base col step operand evac arg")
KINDS = {"wide": (2, 4), "pair": (2, 4), "trio": (2, 3), "narrow": (4, 1)}

DMAS = {"wide": 1, "pair": 2, "trio": 2, "narrow": 1}


def plan_stream():
    blocks, phases = [], {}

    def phase(name, body, bodies=1):
        phases[name] = (len(blocks), len(body), bodies)
        for i in range(bodies):
            blocks.extend(b._replace(col=b.col + i * b.step, arg=b.arg + i * len(body)) for b in body)

    def wide(w, col, n, step, operand, evac, kt=KD):
        return [Block(w, kt, "wide", 0, col + 512 * j, step, operand, evac, j) for j in range(n)]

    def gated(w, gate_col, up, evac):
        return [b for j in range(2) for b in (
            Block(w, KD, "wide", 0, gate_col + 512 * j, 1024, "h", "gate", 2 * j),
            Block(up, KB, "wide", 0, 512 * j, 1024, "y", evac, 2 * j + 1))]

    phase("lora", [Block("w_in", KD, "narrow", 0, LORA_COL, 0, "h", "lora", 0)])
    for p in range(-1, KB):
        if p + 1 < KB:
            phase(f"B{p + 1}", [Block("w_in", KD, "pair", B_COL, P * (p + 1), 0, "h", "rwkv", p + 1)])
        if p >= 0:
            phase(f"A{p}", [Block("w_in", KD, "wide", 0, A_COL + 512 * p, 0, "h", "a_cols", p)])
    phase("gate_b", gated("w_in", GB_COL, "w_up_b", "merge0"), 2)
    phase("C", wide("w_in", C_COL, 4, 0, "h", "c_cols"))
    phase("gate_a", gated("w_in", GA_COL, "w_up_a", "merge"), 2)
    phase("gate_c", wide("w_in", GC_COL, 2, 1024, "h", "gate_c"), 2)
    phase("mem", wide("w_mem_kv", 0, 2, 1024, "h", "mem"), 2)
    phase("up_c", wide("w_up_c", 0, 2, 1024, "y", "merge_c", KB), 2)
    phase("o", wide("w_o", 0, 2, 1024, "h", "residual"), 2)
    phase("Q", wide("w_in_2", Q_COL, 2, 1024, "h", "q_cols"), 3)
    phase("L", wide("w_in_2", L_COL, 6, 0, "h", "l_cols"))
    phase("down", [Block("w_in_2", KD, "narrow", 0, DOWN_COL, 0, "h", "gla_down", 0)])
    phase("gate_1", gated("w_in_2", M_COL, "w_br_attn_2", "merge0"), 2)
    for p in range(KB):
        phase(f"V{p}", [Block("w_in_2", KD, "trio", V_COL, P * p, 0, "h", "conv", p)])
    phase("gate_2", gated("w_in_2", M_COL + 2048, "w_br_gla_2", "merge"), 2)
    phase("gate_3", gated("w_in_2", M_COL + 4096, "w_br_conv_2", "merge"), 2)
    phase("o2", wide("w_out_2", 0, 2, 1024, "h", "residual"), 2)
    phase("ffn", [Block("w_ffn_gate_2", KD, "wide", 0, 0, 512, "h", "ffn_gate", 0),
                  Block("w_ffn_up_2", KD, "wide", 0, 0, 512, "h", "ffn_up", 1)], 11)
    phase("ffn_down", wide("w_ffn_down_2", 0, 2, 1024, "f", "residual", KF), 2)
    units, first = [], []
    for m, b in enumerate(blocks):
        first.append(len(units))
        units.extend((m, u) for u in range(b.kt // KINDS[b.kind][0]))
    return blocks, phases, units, first


ROWS1 = [("norm_g", 16), ("mem_norm_g", 16), ("norm1_w_2", 16), ("norm2_w_2", 16), ("final_norm_w_2", 16)]
ROWS2 = [("b_mu_rkv", 24), ("b_w0", 8), ("b_a0", 8), ("b_k_k", 8), ("b_k_a", 8), ("b_r_k", 8), ("b_ln_w", 8),
         ("b_ln_b", 8), ("a_q_g", 1), ("a_k_g", 1), ("c_q_g", 2), ("c_k_g", 2), ("gla_b_2", 4), ("gla_norm_w_2", 2),
         ("conv_w_2", 24), ("b_mu_w", 1)]


N_ROW_DMAS = len(ROWS1) + len(ROWS2) + 1
HEAD0 = {"a": 0, "c": 8, "q": 12}
TURNS = {"x": 8, "a": 12, "mem": 20, "c": 24, "q": 28, "l": 32, "out": 40}


def build(nc, dram, out):
    blocks, phases, units, first = plan_stream()
    n_units = len(units)
    landed = []
    for n, (m, _) in enumerate(units):
        landed.append((landed[n - RING] if n >= RING else 0) + 16 * DMAS[blocks[m].kind])

    def last_unit(m):
        return first[m + 1] - 1 if m + 1 < len(first) else n_units - 1

    with ExitStack() as ctx:
        sem_of = {}

        def sem(name):
            if name not in sem_of:
                sem_of[name] = ctx.enter_context(nc.semaphore(name))
            return sem_of[name]

        def sb(name, shape, dt=F32, where=ctx):
            return where.enter_context(nc.sbuf_tensor(name, shape, dt))

        w_raw = sb("w_raw", [P, RING, UNIT])
        w_hi = sb("w_hi", [P, RING, UNIT], F32R)
        w_lo = sb("w_lo", [P, RING, UNIT], F32R)
        x_t = sb("x_t", [P, KD, T])
        h_hi = sb("h_hi", [P, KD, T], F32R)
        h_lo = sb("h_lo", [P, KD, T], F32R)
        ident = sb("ident", [P, P])
        ones = sb("ones", [P, P])
        blk = sb("blk", [P, P])
        m_strict = sb("m_strict", [P, P], U8)
        m_incl_t = sb("m_incl_t", [P, P], U8)
        m_strict_t = sb("m_strict_t", [P, P], U8)
        m_gla = sb("m_gla", [P, P], U8)
        m_level = [sb(f"m_level{l}", [P, P // 2], U8) for l in range(LEVELS)]
        m_level_t = [sb(f"m_level_t{l}", [P, P // 2], U8) for l in range(LEVELS)]
        m_work = sb("m_work", [P, P])
        vec1 = sb("vec1", [P, 80])
        vec2 = sb("vec2", [P, 128])
        one_minus_ka = sb("one_minus_ka", [P, KB])
        small = sb("small", [P, 32])
        y_ctx = ExitStack()
        y_hi = sb("y_hi", [P, KB, T], F32R, y_ctx)
        y_lo = sb("y_lo", [P, KB, T], F32R, y_ctx)
        ARENA = 83 * 256
        arena = sb("arena", [P, ARENA], F32, y_ctx)
        y_ctx.close()
        f_hi = sb("f_hi", [P, KF, T], F32R)
        f_lo = sb("f_lo", [P, KF, T], F32R)
        f_t = sb("f_t", [P, 2, UNIT])
        rel = nc.dram_tensor("rel_scratch", (8, 384), F32, kind="Internal")

        def unit_size(n):
            k, tiles = KINDS[blocks[units[n][0]].kind]
            return k * tiles * P

        def area(kb, *shape):
            at, size = int(kb * 256), int(np.prod(shape))
            assert at + size <= ARENA, (kb, shape)
            v = arena[:, at:at + size]
            if len(shape) == 2:
                v = v.rearrange("p (a b) -> p a b", b=shape[1])
            return v

        v1, v2, at = {}, {}, 0
        for name, rows in ROWS1:
            v1[name], at = at, at + rows
        n_rows1, at = at, 0
        for name, rows in ROWS2:
            v2[name], at = at, at + rows
        n_rows2 = at

        def g1(name, t=0):
            return vec1[:, v1[name] + t:v1[name] + t + 1]

        def g2(name, t=0):
            return vec2[:, v2[name] + t:v2[name] + t + 1]

        gp = ctx.enter_context(nc.psum_tensor("gp", [P, 2, UNIT], F32))
        ps = ctx.enter_context(nc.psum_tensor("ps", [P, 4, 512], F32))
        psA, psB, psC, psD = (ps[:, b, :] for b in range(4))
        psCD = ps[:, 2:4, :].rearrange("p a b -> p (a b)")

        x_rows = area(0, 2, D)
        rows1, rows2 = area(16, P), area(16.5, P)
        n_sq = [area(64, UNIT), area(68, UNIT)]
        a_q, a_k, a_vraw, a_z = area(0, KB, T), area(8, KB, T), area(16, KB, T), area(24, KB, T)
        r_raw = [area(32, 4, T + 1), area(36.25, 4, T + 1)]
        lora, lora_x, w2a2 = area(40.5, T + 1), area(41.75, T), area(42.75, BW)
        r_d, r_rkv = area(46.75, 3, T), area(49.75, 3, T)
        r_sg, r_aa, r_kk, r_sq, r_rs = (area(52.75 + j, T) for j in range(5))
        r_cs, r_e1, r_e2 = (area(57.75 + 1.125 * j, 2, CHUNK + 1) for j in range(3))
        r_at, r_bt, r_kt, r_rt, r_rk = (area(61.25 + j, T) for j in range(5))
        r_cm, r_x, r_xt, r_g, r_ak, r_arb, r_ark, r_vbk = (area(66.25 + 2 * j, 4, P) for j in range(8))
        r_s = area(82.25, 64)
        r_w, r_u = r_sg, r_sq
        r_o, r_dd, r_t, r_o2, r_af = r_kk, r_rs, r_d[:, 0, :], r_d[:, 1, :], r_d[:, 2, :]
        mg, sig, prod = area(32, KD * T), area(48, UNIT), area(52, UNIT)
        att_v = area(56, 2, BW)
        att_s, att_pt, att_t = [area(48, 2, T), area(50, 2, T)], area(52, 2, T), area(54, 2 * T)
        a_bias, a_hankel = [area(64, 2, T), area(66, 2, T)], [area(68, T), area(69, T)]
        ext = area(70, 384)[0:8, :]
        hn_sq, hn_rs = area(64, UNIT), area(68, UNIT)
        c_q, c_z = area(72, KB, T), area(16, KB, T)
        sig_c = area(0, 4 * UNIT)
        mem_rows = [area(56, D), area(64, D)]
        mem_t = [area(48, UNIT), area(52, UNIT)]
        c_k, c_vraw, c_v = area(24, KB, T), area(56, KB, T), area(64, 2, BW)
        c_sq, c_rs = area(48, UNIT), area(52, UNIT)
        c_bias = area(80, 2, T)
        q_all = area(0, 3 * 2 * UNIT)
        q_q, q_k, q_vraw = area(0, KB, T), area(8, KB, T), area(16, KB, T)
        q_bias, q_dist = [area(32, 2, T), area(34, 2, T)], area(36, 2, T)
        l_q, l_k, l_vraw, l_z = area(24, 4, T), area(28, 4, T), area(64, KB, T), area(72, KB, T)
        l_down, l_up, l_v = area(80, T), area(81, 512), area(56, 2, BW)
        v_raw = [area(0, 3, T), area(3, 3, T)]
        v_cu, v_y, v_t = area(6, T + 2), area(8, KB, T), area(7.125, 128 + 64)
        v_t = area(16, T)
        l_t1, l_t2, l_cs, l_e1, l_e2, l_qin, l_kin = (area(17 + j, T) for j in range(7))
        l_at, l_kt, l_sq = area(64, 2, P), area(65, 2, P), area(66, 2, T)
        l_s = [area(68 + j, T) for j in range(3)]
        l_y = area(48, 2 * T)
        l_rs = area(50, T)

        def one_of_pair(v, l, e):
            return v[:, :, :].rearrange("p a (b e w) -> p a b e w", e=2, w=1 << l)[:, :, :, e, :]

        def packed(v, l):
            return v[:, 0:4 * P // 2].rearrange("p (a b w) -> p a b w", a=4, w=1 << l)

        def level_mask(v, l):
            return v[:].rearrange("p (b w) -> p b w", w=1 << l).unsqueeze(1).to_broadcast([P, 4, P // (2 << l), 1 << l])

        def mask4(v, n=4):
            return v[:].unsqueeze(1).to_broadcast([P, n, P])

        block = ctx.enter_context(nc.Block())

        class Seen:

            def __init__(self, eng):
                self.eng, self.n = eng, Counter()

            def need(self, name, k=1):
                self.n[name] += k
                self.eng.wait_ge(sem(name), self.n[name])

            def skip(self, name, k=1):
                self.n[name] += k

        def on(i, const, each):
            return const if i is None else i * each + const

        def wait_evacuated(eng, m, i=None, body=0):
            eng.wait_ge(sem(f"evacuated{m % 2}"), on(i, m // 2 + 1, body // 2))

        def run(eng, unit, name, straight=()):
            m0, body, bodies = phases[name]
            n0 = first[m0]
            per = (first[m0 + body] if m0 + body < len(first) else n_units) - n0
            loops = bodies > 1 and name not in straight and name not in ("mem", "gate_1", "ffn_down", list(phases)[-1])
            if not loops:
                for n in range(n0, n0 + per * bodies):
                    unit(n)
                return
            with eng.Fori(0, bodies) as i:
                for n in range(n0, n0 + per):
                    unit(n, i, per, body)

        def filler(unit, names):
            todo = [n for name in names for n in range(first[phases[name][0]], last_unit(phases[name][0] + phases[name][1] * phases[name][2] - 1) + 1)]

            def fill(k=1):
                for _ in range(k):
                    if todo:
                        unit(todo.pop(0))
            fill.drain = lambda: fill(len(todo))
            return fill

        def source(b, u, col):
            per = KINDS[b.kind][0]
            w = dram[b.weight].rearrange("l (k p) n -> (l k) p n", p=P).rearrange("k p n -> p k n")
            w = w[:, per * u:per * u + per, :]
            if b.kind == "narrow":
                return w[:, :, b.col:b.col + 128]
            if b.kind == "wide":
                return w[:, :, bass.ds(col, 512)]
            q = KINDS[b.kind][1]
            return w[:, :, b.base:b.base + 1024 * q].rearrange("p k (q c) -> p k q c", q=q)[:, :, :, b.col:b.col + P]

        @block.sync
        def _(sp):
            x_in = dram["x"].rearrange("b (a p) d -> (b a) p d", p=P)
            for a in range(2):
                sp.dma_start(x_rows[:, a, :], x_in[a]).then_inc(sem(f"x_landed{a}"), 16)
            for name, rows in ROWS1:
                src = dram[name]
                src = src.rearrange("l (r c) -> (l r) c", c=P) if len(src.shape) == 2 else src.rearrange("(r c) -> r c", c=P)
                sp.dma_start(rows1[v1[name]:v1[name] + rows, :], src).then_inc(sem("rows_landed"), 16)
            n_dma = len(ROWS1)
            for name, rows in ROWS2:
                at = v2[name]
                if name == "b_mu_w":
                    sp.dma_start(rows2[at:at + 1, 0:64], dram["b_mu_w"]).then_inc(sem("rows_landed"), 16)
                    sp.dma_start(rows2[at:at + 1, 64:128], dram["b_mu_a"]).then_inc(sem("rows_landed"), 16)
                    n_dma += 2
                    continue
                src = dram[name]
                if name == "b_r_k":
                    src = src.rearrange("l h d -> l (h d)")
                src = src.rearrange("l k (r c) -> (l k r) c", c=P) if len(src.shape) == 3 else src.rearrange("l (r c) -> (l r) c", c=P)
                sp.dma_start(rows2[at:at + rows, :], src).then_inc(sem("rows_landed"), 16)
                n_dma += 1
            assert n_dma == N_ROW_DMAS

            def unit(n, i=None, per=0, body=0):
                m, u = units[n]
                b, slot = blocks[m], n % RING
                col = b.col if i is None else i * b.step + b.col
                if n >= RING:
                    sp.wait_ge(sem("lo_done"), on(i, n - RING + 1, per))
                k, tiles = KINDS[b.kind]
                dst = w_raw[:, slot, 0:k * tiles * P].rearrange("p (k n) -> p k n", k=k)
                if DMAS[b.kind] == 1:
                    sp.dma_start(dst, source(b, u, col)).then_inc(sem(f"landed{slot}"), 16)
                    return
                for j in range(k):
                    sp.dma_start(dst[:, j, :].rearrange("p (q c) -> p q c", q=tiles), source(b, u, col)[:, j])\
                        .then_inc(sem(f"landed{slot}"), 16)

            first_units = filler(unit, ["lora"])
            first_units.drain()
            sp.dma_start(w2a2[0:64, :], dram["b_w2"].rearrange("l k n -> (l k) n")).then_inc(sem("w2_landed"), 16)
            sp.dma_start(w2a2[64:128, :], dram["b_a2"].rearrange("l k n -> (l k) n")).then_inc(sem("w2_landed"), 16)
            for name in phases:
                if name != "lora":
                    run(sp, unit, name, straight=("gate_b", "gate_a", "gate_2", "gate_3"))
            out_rows = out.rearrange("b (a p) d -> (b a) p d", p=P)
            for a in range(2):
                sp.wait_ge(sem("turn_copied"), TURNS["l"] + 4 * a + 4)
                sp.dma_start(out_rows[a], x_rows[:, a, :]).then_inc(sem("out_stored"), 16)
            sp.wait_ge(sem("out_stored"), 32)

        @block.gpsimd
        def _(pool):
            seen = Seen(pool)

            def link(ins):
                ins.then_inc(sem("pool_step"), 1)
                seen.need("pool_step")

            pool.memset(ident[:], 0.0)
            link(pool.memset(small[:], 0.0))
            link(pool.memset(small[:, 24:25], EPS))
            link(pool.memset(small[:, 25:26], GN_EPS))
            pool.affine_select(out=ident[:], in_=ident[:], compare_op=ALU.not_equal, fill=1.0, base=0,
                               pattern=[[-1, P]], channel_multiplier=1).then_inc(sem("ident_ready"), 1)
            pool.memset(ones[:], 1.0)
            link(pool.memset(blk[:], 0.0))
            link(pool.memset(blk[0:64, 0:64], 1.0))
            pool.memset(blk[64:128, 64:128], 1.0).then_inc(sem("ones_ready"), 1)
            pool.wait_ge(sem("ones_ready"), 1)
            for r in r_raw:
                pool.memset(r[:, :, 0:1], 0.0)
            pool.memset(lora[:, 0:1], 0.0)
            pool.memset(r_cs[:, :, 0:1], 0.0).then_inc(sem("zeros_ready"), 1)

            def mask(dst, *selects):
                work = m_work[:, 0:dst.shape[1]]
                link(pool.memset(work, 0.0))
                for k, (view, op, base, pattern, mult) in enumerate(selects):
                    v = view(work)
                    if op in (ALU.is_le, ALU.is_lt):
                        op = {ALU.is_le: ALU.is_ge, ALU.is_lt: ALU.is_gt}[op]
                        base, mult, pattern = -base, -mult, [[-step, count] for step, count in pattern]
                    link(pool.affine_select(out=v, in_=v, compare_op=op, fill=0.0 if k else 1.0, base=base,
                                            pattern=pattern, channel_multiplier=mult))
                link(pool.tensor_copy(dst[:], work))

            whole = lambda w: w
            mask(m_strict, (whole, ALU.is_le, 0, [[-1, P]], 1))
            mask(m_strict_t, (whole, ALU.is_le, 0, [[1, P]], -1))
            mask(m_incl_t, (whole, ALU.is_lt, 0, [[1, P]], -1))
            halves = lambda w: w.rearrange("p (b w) -> p b w", w=64)
            mask(m_gla, (whole, ALU.is_lt, 0, [[1, P]], -1), (halves, ALU.is_ge, 0, [[-64, 2], [0, 64]], 1))
            for l in range(LEVELS):
                w = 1 << l
                pairs = lambda v: v.rearrange("p (b w) -> p b w", w=w)
                pattern = [[-2 * w, P // (2 * w)], [0, w]]
                mask(m_level[l], (pairs, ALU.is_lt, -w, pattern, 1), (pairs, ALU.is_lt, -2 * w, pattern, 1))
                mask(m_level_t[l], (pairs, ALU.is_lt, 0, pattern, 1), (pairs, ALU.is_lt, -w, pattern, 1))
            pool.wait_ge(sem("norm_lo"), 4)
            pool.memset(r_g[:, :, :], 0.0)
            for z in (r_cm, r_ak, r_arb):
                pool.memset(z[:, :, :], 0.0)
            pool.memset(r_ark[:, :, :], 0.0).then_inc(sem("masks_ready"), 1)

            for p in range(KB):
                wait_evacuated(pool, phases[f"B{p}"][0])
                if p:
                    pool.wait_ge(sem("shift_read"), p)
                    pool.wait_ge(sem("y_lo"), p)
                raw = r_raw[p % 2]
                pool.tensor_tensor(r_d[:, :, :], raw[:, 0:3, 0:T], raw[:, 0:3, 1:T + 1], ALU.subtract)\
                    .then_inc(sem("shift_ready"), 1)
                for t in range(4):
                    pool.tensor_copy(r_x[:, t, :], ident[:])
                    ins = pool.tensor_copy(r_xt[:, t, :], ident[:])
                ins.then_inc(sem("inverse_reset"), 1)

            pool.wait_ge(sem("hn_done"), 4)
            pool.dma_start(ext[:, 0:256], dram["a_rel_bias"].rearrange("l h r -> (l h) r")[:, 1:257]).then_inc(sem("ext_landed"), 16)
            pool.wait_ge(sem("ext_landed"), 16)
            link(pool.tensor_scalar(ext[:, 256:384], ones[0:8, :], ext[:, 255:256], None, ALU.mult))
            pool.dma_start(rel.ap(), ext).then_inc(sem("rel_stored"), 16)
            pool.wait_ge(sem("rel_stored"), 16)
            h0 = HEAD0["a"]
            for h in range(8):
                if h >= 2:
                    pool.wait_ge(sem("scores_read"), h0 + h - 1)
                hank, bias = a_hankel[h % 2], a_bias[h % 2]
                src = bass.AP(rel, h * 384, [[1, P], [1, T]])
                pool.dma_start(hank, src).then_inc(sem(f"hankel_landed{h % 2}"), 16)
                pool.wait_ge(sem(f"hankel_landed{h % 2}"), 16 * (h // 2 + 1))
                pool.tensor_copy(bias[:, 0, 0:P], hank[:, 0:P][:, ::-1])
                pool.memset(bias[:, 0, P:T], MASKED)
                link(pool.tensor_copy(bias[:, 1, :], hank[:, ::-1]))
                link(pool.memset(bias[0:64, 0, 64:P], MASKED))
                pool.memset(bias[0:64, 1, 192:T], MASKED).then_inc(sem("bias_ready"), 1)
                pool.wait_ge(sem("bias_ready"), h + 1)
            pool.wait_ge(sem("y_lo"), HEAD0["a"] + 8 + KB)
            for a in range(2):
                pool.dma_start(mem_rows[a], dram["mem"].rearrange("b (a p) d -> (b a) p d", p=P)[a])\
                    .then_inc(sem(f"mem_landed{a}"), 16)
            pool.memset(c_bias[:, :, :], 0.0).then_inc(sem("c_bias_ready"), 1)
            pool.wait_ge(sem("norm_lo"), 8)
            pool.dma_start(l_up[0:16, :], dram["gla_w_up_2"].rearrange("l r n -> (l r) n")).then_inc(sem("up_landed"), 16)
            link(pool.iota(q_dist[:, :, :], pattern=[[-P, 2], [1, T]], base=0, channel_multiplier=-1,
                           allow_small_or_imprecise_dtypes=True))
            link(pool.affine_select(out=q_dist[:, :, :], in_=q_dist[:, :, :], compare_op=ALU.is_ge, fill=MASKED,
                                    base=0, pattern=[[P, 2], [-1, T]], channel_multiplier=1))
            h0 = HEAD0["q"]
            for h in range(8):
                if h >= 2:
                    pool.wait_ge(sem("scores_read"), h0 + h - 1)
                pool.tensor_scalar(q_bias[h % 2][:, :, :], q_dist[:, :, :], 2.0 ** -(h + 1), None, ALU.mult)\
                    .then_inc(sem("bias_ready"), 1)
            pool.wait_ge(sem("turn_copied"), TURNS["l"])
            pool.memset(l_at[:, :, :], 0.0)
            pool.memset(v_cu[:, 0:2], 0.0).then_inc(sem("gla_zeros"), 1)

        @block.scalar
        def _(act):
            seen = Seen(act)

            def root(dst, src, eps=EPS):
                at = {EPS: 24, GN_EPS: 25, 0.0: 26}[eps]
                act.activation(dst, src, ACT.Sqrt, bias=small[:, at:at + 1]).then_inc(sem("root_ready"), 1)

            def hi(n, i=None, per=0):
                slot = n % RING
                if n >= RING:
                    act.wait_ge(sem("unit_used"), on(i, n - RING + 1, per))
                act.wait_ge(sem(f"landed{slot}"), on(i, landed[n], 16 * per // RING))
                size = unit_size(n)
                act.activation(w_hi[:, slot, 0:size], w_raw[:, slot, 0:size], ACT.Copy).then_inc(sem("hi_done"), 1)

            def flat(v, at, i, each, size=UNIT):
                return v[:, at:at + size] if i is None else v[:, bass.ds(i * each + at, size)]

            def evacuate(m, i, per, body):
                b, g = blocks[m], gp[:, m % 2, :]
                done = sem(f"evacuated{m % 2}")
                kind, a = b.evac, b.arg
                if kind == "merge_c":
                    merged_high(a, 0, i, body)
                if kind in ("merge0", "merge", "merge_c", "residual"):
                    return
                act.wait_ge(sem("unit_used"), on(i, last_unit(m) + 1, per))
                tiles = g.rearrange("p (a b) -> p a b", b=T)
                if kind == "lora":
                    act.activation(lora[:, 1:T + 1], g[:, 0:T], ACT.Copy).then_inc(done, 1)
                elif kind == "rwkv":
                    if a >= 2:
                        act.wait_ge(sem("y_lo"), a - 1)
                    raw = r_raw[a % 2]
                    act.activation(raw[:, 0:3, 1:T + 1], tiles[:, 0:3, :], ACT.Copy)
                    act.activation(raw[:, 3, 1:T + 1], tiles[:, 3, :], ACT.Silu).then_inc(done, 1)
                elif kind == "a_cols":
                    dst = (a_q, a_k, a_vraw, a_z)[a // 2][:, 4 * (a % 2):4 * (a % 2) + 4, :]
                    act.activation(dst, tiles, ACT.Silu if a >= 6 else ACT.Copy).then_inc(done, 1)
                elif kind == "c_cols":
                    dst = (c_q, c_z)[a // 2][:, 4 * (a % 2):4 * (a % 2) + 4, :]
                    act.activation(dst, tiles, ACT.Silu if a >= 2 else ACT.Copy).then_inc(done, 1)
                elif kind == "l_cols":
                    dst = (l_q[:, :, :], l_k[:, :, :], l_vraw[:, 0:4, :], l_vraw[:, 4:8, :], l_z[:, 0:4, :], l_z[:, 4:8, :])[a]
                    act.activation(dst, tiles, ACT.Silu if a >= 4 else ACT.Copy).then_inc(done, 1)
                elif kind == "mem":
                    dst = (c_k, c_vraw)[a // 2][:, 4 * (a % 2):4 * (a % 2) + 4, :]
                    act.activation(dst, tiles, ACT.Copy).then_inc(done, 1)
                elif kind == "gla_down":
                    act.activation(l_down, g[:, 0:T], ACT.Copy).then_inc(done, 1)
                elif kind == "conv":
                    if a >= 2:
                        act.wait_ge(sem("conv_done"), a - 1)
                    act.activation(v_raw[a % 2][:, :, :], tiles[:, 0:3, :], ACT.Copy).then_inc(done, 1)
                elif kind == "gate":
                    wait_evacuated(act, m - 1, i, body)
                    act.activation(sig, g, ACT.Sigmoid).then_inc(done, 1)
                elif kind == "gate_c":
                    act.activation(flat(sig_c, a * UNIT, i, body * UNIT), g, ACT.Sigmoid).then_inc(done, 1)
                elif kind == "q_cols":
                    act.activation(flat(q_all, a * UNIT, i, body * UNIT), g, ACT.Copy).then_inc(done, 1)
                elif kind == "ffn_gate":
                    wait_evacuated(act, m - 1, i, body)
                    act.activation(f_t[:, 0, :], g, ACT.Silu).then_inc(done, 1)
                elif kind == "ffn_up":
                    act.wait_ge(sem("ffn_prod"), on(i, 1, 1))
                    dst = f_hi[:].rearrange("p a b -> p (a b)")
                    act.activation(flat(dst, 0, i, UNIT), f_t[:, 1, :], ACT.Copy).then_inc(sem("ffn_hi"), 1)

            def merged_high(q, before, i, each):
                act.wait_ge(sem("added"), on(i, 2 * before + 4 + q + 1, each))
                at = q * UNIT
                act.activation(flat(h_hi[:].rearrange("p a b -> p (a b)"), at, i, each * UNIT), flat(mg, at, i, each * UNIT), ACT.Copy)\
                    .then_inc(sem("merged_hi"), 1)

            def unit(n, i=None, per=0, body=0):
                if n + LEAD < n_units:
                    hi(n + LEAD, i, per)
                m, _ = units[n]
                if n == last_unit(m):
                    evacuate(m, i, per, body)

            def norm():
                for q in range(4):
                    if q >= 2:
                        act.wait_ge(sem("norm_sq_used"), act_n["norm"] * 4 + q - 1)
                    act.activation(n_sq[q % 2], x_t[:, 4 * q:4 * q + 4, :].rearrange("p a b -> p (a b)"), ACT.Square,
                                   scale=D ** -0.5).then_inc(sem("norm_sq"), 1)
                act_n["norm"] += 1
                act.wait_ge(sem("norm_sq_used"), 4 * act_n["norm"])
                root(area(76, T), psC[:, 0:T])

            act_n = Counter()

            def split(h_dst, src, ready, done, quarters=4):
                for q in range(quarters):
                    seen.need(ready)
                    act.activation(h_dst(q), src(q), ACT.Copy).then_inc(sem(done), 1)

            def h_part(v):
                return lambda q: v[:, 4 * q:4 * q + 4, :].rearrange("p a b -> p (a b)")

            def heads_norm(src, size, buf, rs, ready):
                for half in range(2):
                    ready(half)
                    if act_n["hn"]:
                        act.wait_ge(sem("hn_sq_used"), act_n["hn"])
                    act_n["hn"] += 1
                    act.activation(buf, src[:, 4 * half:4 * half + 4, :].rearrange("p a b -> p (a b)"), ACT.Square,
                                   scale=size ** -0.5).then_inc(sem("hn_sq"), 1)
                    act.wait_ge(sem("hn_sq_used"), act_n["hn"])
                    if act_n["hn"] > 1:
                        act.wait_ge(sem("hn_done"), act_n["hn"] - 1)
                    w = UNIT * 128 // size
                    root(rs[:, 0:w], psCD[:, 0:w])

            def attention(which, n_heads, dt, fill, fills):
                h0 = HEAD0[which]
                for h in range(n_heads + 1):
                    if h < n_heads:
                        g = h0 + h
                        act.wait_ge(sem("max_ready"), g + 1)
                        s = att_s[g % 2]
                        for tt in range(2):
                            k = 2 * (g % 2) + tt
                            ins = act.activation(s[:, tt, :], s[:, tt, :], ACT.Exp, bias=small[:, k:k + 1],
                                                 accum_out=small[:, 4 + k:5 + k])
                        ins.then_inc(sem("exp_done"), 1)
                    if h:
                        split_y(g0=h - 1, dt=dt)
                    fill(fills)

            def split_y(g0, dt):
                seen.need("y_t")
                act.activation(y_hi[:, g0 * dt:g0 * dt + dt, :].rearrange("p a b -> p (a b)"), att_t[:, 0:dt * T],
                               ACT.Copy).then_inc(sem("y_hi"), 1)

            def pair(p, fill):
                e = p
                act.wait_ge(sem("lora_z"), p + 1)
                act.activation(r_sg, psA[:, 0:T], ACT.Sigmoid, bias=g2("b_w0", p))
                act.activation(r_aa, psA[:, T:2 * T], ACT.Sigmoid, bias=g2("b_a0", p)).then_inc(sem("sigmoids"), 1)
                fill()
                act.wait_ge(sem("kk_ready"), p + 1)
                act.activation(r_sq, r_kk, ACT.Square).then_inc(sem("kk_sq"), 1)
                fill()
                act.wait_ge(sem("kk_sum"), p + 1)
                root(r_rs, psB[:, 0:T], 0.0)
                act.wait_ge(sem("mid_ready"), p + 1)
                for c in range(2):
                    act.activation(r_e1[:, c, :], r_cs[:, c, :], ACT.Exp, bias=small[:, 16 + c:17 + c], scale=-KAPPA)
                    ins = act.activation(r_e2[:, c, :], r_cs[:, c, :], ACT.Exp, bias=small[:, 18 + c:19 + c], scale=KAPPA)
                ins.then_inc(sem("decays"), 1)
                fill(3)
                for l in range(1, LEVELS):
                    act.wait_ge(sem("g_done"), p * (LEVELS - 1) + l)
                    act.activation(one_of_pair(r_g, l, 1), packed(psB, l), ACT.Copy).then_inc(sem("g_read"), 1)
                    fill()
                fill(2)
                act.wait_ge(sem("o_done"), p + 1)
                act.activation(r_o, psB[:, 0:T], ACT.Copy).then_inc(sem("o_read"), 1)
                fill()
                act.wait_ge(sem("dev_ready"), p + 1)
                act.activation(r_sq, r_dd, ACT.Square, scale=1.0 / 8).then_inc(sem("dev_sq"), 1)
                act.wait_ge(sem("var_done"), p + 1)
                root(r_aa, psC[:, T:2 * T], GN_EPS)
                fill()
                act.wait_ge(sem("rwkv_t"), p + 1)
                act.activation(y_hi[:, p, :], r_t, ACT.Copy).then_inc(sem("y_hi"), 1)

            for n in range(LEAD):
                hi(n)
            act.wait_ge(sem("turn_copied"), TURNS["x"])
            norm()
            split(h_part(h_hi), lambda q: n_sq[q % 2], "norm_t", "norm_hi")
            lo = filler(unit, ["lora", "B0"])
            lo.drain()
            act.wait_ge(sem("lora_shifted"), 1)
            act.activation(lora_x[0:64, :], lora_x[0:64, :], ACT.Tanh).then_inc(sem("lora_ready"), 1)
            for p in range(KB):
                fill = filler(unit, ([f"B{p + 1}"] if p + 1 < KB else []) + [f"A{p}"])
                pair(p, fill)
                fill.drain()
            fill = filler(unit, ["gate_b"])
            for src, m in ((a_q, "A1"), (a_k, "A3")):
                heads_norm(src, 128, hn_sq, hn_rs, lambda half: None)
                fill(4)
            fill.drain()
            fill = filler(unit, ["C"])
            attention("a", 8, 1, fill, 4)
            fill.drain()
            run(act, unit, "gate_a")
            run(act, unit, "gate_c")
            act.wait_ge(sem("added"), 4)
            for a in range(2):
                act.wait_ge(sem(f"mem_landed{a}"), 16)
                for q in range(2):
                    if a:
                        act.wait_ge(sem("mem_sums"), q + 1)
                    act.activation(mem_t[q], mem_rows[a][:, q * UNIT:(q + 1) * UNIT], ACT.Square, scale=D ** -0.5,
                                   accum_out=small[:, 20 + 2 * a + q:21 + 2 * a + q]).then_inc(sem("mem_sums"), 1)
            act.wait_ge(sem("mem_mean"), 1)
            root(small[:, 28:30], small[:, 28:30])
            act.wait_ge(sem("unit_used"), first[phases["mem"][0]])
            for q in range(4):
                act.wait_ge(sem("turn_copied"), TURNS["a"] + 2 * q + 2)
                act.activation(h_part(h_hi)(q), mem_t[q % 2], ACT.Copy).then_inc(sem("mem_hi"), 1)
            run(act, unit, "mem")
            wait_evacuated(act, phases["mem"][0])
            heads_norm(c_q, 256, c_sq, c_rs, lambda half: None)
            heads_norm(c_k, 256, c_sq, c_rs, lambda half: wait_evacuated(act, phases["mem"][0] + half))
            attention("c", 4, 2, lambda k: None, 0)
            run(act, unit, "up_c")
            run(act, unit, "o")
            wait_evacuated(act, phases["Q"][0] - 1)
            wait_evacuated(act, phases["Q"][0] - 2)
            norm()
            split(h_part(h_hi), lambda q: n_sq[q % 2], "norm_t", "norm_hi")
            run(act, unit, "Q")
            fill = filler(unit, ["L", "down"])
            attention("q", 8, 1, fill, 6)
            fill.drain()
            run(act, unit, "gate_1")
            fill = filler(unit, [f"V{p}" for p in range(KB)])
            for h in range(4):
                act.wait_ge(sem("gla_min"), h + 1)
                act.activation(l_t1, psA[:, 0:T], ACT.Abs, bias=g2("gla_b_2", h)).then_inc(sem("act_step"), 1)
                seen.need("act_step")
                act.activation(l_t1, l_t1, ACT.Exp, scale=-1.0).then_inc(sem("act_step"), 1)
                seen.need("act_step")
                act.activation(l_t1, l_t1, ACT.Ln, bias=1.0).then_inc(sem("gla_ln"), 1)
                fill(4)
                act.wait_ge(sem("gla_cs"), h + 1)
                act.activation(l_e1, l_cs, ACT.Exp, scale=1.0 / 16)
                act.activation(l_e2, l_cs, ACT.Exp, scale=-1.0 / 16).then_inc(sem("gla_decays"), 1)
                fill(4)
                act.wait_ge(sem("gla_o"), h + 1)
                act.activation(l_sq[:, :, :].rearrange("p a b -> p (a b)"), psC, ACT.Square, scale=1.0 / 16).then_inc(sem("gla_sq"), 1)
                fill(4)
                act.wait_ge(sem("gla_ss"), h + 1)
                root(l_rs, psD[:, 0:T])
                seen.need("gla_y")
                act.activation(y_hi[:, 2 * h:2 * h + 2, :].rearrange("p a b -> p (a b)"), l_y, ACT.Copy).then_inc(sem("y_hi"), 1)
                fill(4)
            fill.drain()
            run(act, unit, "gate_2")
            act.wait_ge(sem("unit_used"), last_unit(phases["gate_3"][0] - 1) + 1)
            for q in range(2):
                act.wait_ge(sem("conv_done"), 4 * q + 4)
                act.activation(y_hi[:, 4 * q:4 * q + 4, :].rearrange("p a b -> p (a b)"),
                               v_y[:, 4 * q:4 * q + 4, :].rearrange("p a b -> p (a b)"), ACT.Copy).then_inc(sem("y_hi"), 1)
            run(act, unit, "gate_3")
            for q in range(4):
                merged_high(q, 4, None, 0)
            run(act, unit, "o2")
            wait_evacuated(act, phases["ffn"][0] - 1)
            wait_evacuated(act, phases["ffn"][0] - 2)
            norm()
            split(h_part(h_hi), lambda q: n_sq[q % 2], "norm_t", "norm_hi")
            run(act, unit, "ffn")
            run(act, unit, "ffn_down")
            wait_evacuated(act, len(blocks) - 1)
            wait_evacuated(act, len(blocks) - 2)
            norm()

        @block.vector
        def _(dve):
            seen = Seen(dve)

            def link(ins):
                ins.then_inc(sem("dve_step"), 1)
                seen.need("dve_step")

            def inverse_root(dst, least=None):
                seen.need("root_ready")
                if least is not None:
                    link(dve.tensor_scalar(dst, dst, least, None, ALU.max))
                link(dve.reciprocal(dst, dst))

            def lo(n, i=None, per=0):
                slot = n % RING
                dve.wait_ge(sem("hi_done"), on(i, n + 1, per))
                size = unit_size(n)
                dve.tensor_tensor(w_lo[:, slot, 0:size], w_raw[:, slot, 0:size], w_hi[:, slot, 0:size].bitcast(F32), ALU.subtract)\
                    .then_inc(sem("lo_done"), 1)

            def flat(v, at, i, each, size=UNIT):
                return v[:, at:at + size] if i is None else v[:, bass.ds(i * each + at, size)]

            def evacuate(m, i, per, body):
                b, g = blocks[m], gp[:, m % 2, :]
                done = sem(f"evacuated{m % 2}")
                kind, a = b.evac, b.arg
                if kind in ("merge0", "merge", "merge_c", "residual", "ffn_up"):
                    dve.wait_ge(sem("unit_used"), on(i, last_unit(m) + 1, per))
                if kind in ("merge0", "merge"):
                    wait_evacuated(dve, m - 1, i, body)
                    each = body // 2 * UNIT
                    if kind == "merge0":
                        dve.tensor_tensor(flat(mg, a // 2 * UNIT, i, each), sig, g, ALU.mult).then_inc(done, 1)
                        return
                    dve.tensor_tensor(prod, sig, g, ALU.mult).then_inc(done, 1)
                    wait_evacuated(dve, m, i, body)
                    part = flat(mg, a // 2 * UNIT, i, each)
                    dve.tensor_tensor(part, part, prod, ALU.add).then_inc(sem("added"), 1)
                elif kind == "merge_c":
                    each = body * UNIT
                    dve.tensor_tensor(prod, flat(sig_c, a * UNIT, i, each), g, ALU.mult).then_inc(done, 1)
                    wait_evacuated(dve, m, i, body)
                    part = flat(mg, a * UNIT, i, each)
                    dve.tensor_tensor(part, part, prod, ALU.add).then_inc(sem("added"), 1)
                    merged_low(a, 0, i, body)
                elif kind == "residual":
                    part = flat(x_t[:].rearrange("p a b -> p (a b)"), a * UNIT, i, body * UNIT)
                    dve.tensor_tensor(part, part, g, ALU.add).then_inc(done, 1)
                elif kind == "ffn_up":
                    wait_evacuated(dve, m - 1, i, body)
                    dve.tensor_tensor(f_t[:, 1, :], f_t[:, 0, :], g, ALU.mult).then_inc(sem("ffn_prod"), 1)
                    dve.wait_ge(sem("ffn_hi"), on(i, 1, 1))
                    hi_part = flat(f_hi[:].rearrange("p a b -> p (a b)"), 0, i, UNIT)
                    lo_part = flat(f_lo[:].rearrange("p a b -> p (a b)"), 0, i, UNIT)
                    dve.tensor_tensor(lo_part, f_t[:, 1, :], hi_part.bitcast(F32), ALU.subtract).then_inc(done, 1)
                elif kind == "conv":
                    wait_evacuated(dve, m)
                    if a == 0:
                        dve.wait_ge(sem("gla_zeros"), 1)
                    raw = v_raw[a % 2]
                    link(dve.tensor_tensor(v_cu[:, 2:T + 2], raw[:, 1, :], raw[:, 2, :], ALU.mult))
                    link(dve.tensor_scalar(v_t, v_cu[:, 0:T], g2("conv_w_2", a), None, ALU.mult))
                    link(dve.scalar_tensor_tensor(v_t, v_cu[:, 1:T + 1], g2("conv_w_2", 8 + a), v_t, ALU.mult, ALU.add))
                    link(dve.scalar_tensor_tensor(v_t, v_cu[:, 2:T + 2], g2("conv_w_2", 16 + a), v_t, ALU.mult, ALU.add))
                    dve.tensor_tensor(v_y[:, a, :], v_t, raw[:, 0, :], ALU.mult).then_inc(sem("conv_done"), 1)

            def merged_low(q, before, i, each):
                dve.wait_ge(sem("merged_hi"), on(i, before + q + 1, each))
                at = q * UNIT
                hi_part = flat(h_hi[:].rearrange("p a b -> p (a b)"), at, i, each * UNIT)
                lo_part = flat(h_lo[:].rearrange("p a b -> p (a b)"), at, i, each * UNIT)
                dve.tensor_tensor(lo_part, flat(mg, at, i, each * UNIT), hi_part.bitcast(F32), ALU.subtract).then_inc(sem("merged_lo"), 1)

            def unit(n, i=None, per=0, body=0):
                if n + LEAD < n_units:
                    lo(n + LEAD, i, per)
                m, _ = units[n]
                if n == last_unit(m):
                    if blocks[m].evac in ("merge", "merge_c"):
                        dve.wait_ge(sem("lo_done"), on(i, n + LEAD + 1, per))
                    evacuate(m, i, per, body)

            dve_n = Counter()

            def turn(dsts):
                for dst in dsts:
                    seen.need("turned")
                    dve.tensor_copy(dst, ps[:, (seen.n["turned"] - 1) % 2, :]).then_inc(sem("turn_copied"), 1)

            def norm(gain, last=False):
                rs = area(76, T)
                inverse_root(rs)

                def scaled(q):
                    for t in range(4):
                        src = x_t[:, 4 * q + t, :]
                        dst = src if last else n_sq[q % 2][:, t * T:(t + 1) * T]
                        ins = dve.scalar_tensor_tensor(dst, src, g1(gain, 4 * q + t), rs, ALU.mult, ALU.mult)
                    ins.then_inc(sem("norm_t"), 1)

                def low(q):
                    seen.need("norm_hi")
                    h = h_hi[:, 4 * q:4 * q + 4, :].rearrange("p a b -> p (a b)")
                    l = h_lo[:, 4 * q:4 * q + 4, :].rearrange("p a b -> p (a b)")
                    dve.tensor_tensor(l, n_sq[q % 2], h.bitcast(F32), ALU.subtract).then_inc(sem("norm_lo"), 1)

                for q in range(4):
                    if q >= 2 and not last:
                        dve.wait_ge(sem("norm_lo"), dve_n["norm_lo"] + q - 1)
                    scaled(q)
                    if q and not last:
                        low(q - 1)
                if not last:
                    low(3)
                dve_n["norm_lo"] += 4

            def heads_norm(dst, gain, per_head, rs):
                for half in range(2):
                    w = 4 // per_head * T
                    inverse_root(rs[:, 0:w])
                    for t in range(4):
                        v = dst[:, 4 * half + t, :]
                        r = rs[:, t // per_head * T:(t // per_head + 1) * T]
                        ins = dve.scalar_tensor_tensor(v, v, g2(gain, t % per_head), r, ALU.mult, ALU.mult)
                    ins.then_inc(sem("hn_done"), 1)

            def attention(which, n_heads, dt, biases, z, fill, fills):
                h0 = HEAD0[which]
                scale = (dt * P) ** -0.5

                def scores(h):
                    g = h0 + h
                    s, k = att_s[g % 2], 2 * (g % 2)
                    dve.wait_ge(sem("scores_done"), g + 1)
                    if which == "c":
                        dve.wait_ge(sem("c_bias_ready"), 1)
                    else:
                        dve.wait_ge(sem("bias_ready"), g + 1 - (4 if which == "q" else 0))
                    dve.scalar_tensor_tensor(s[:, :, :].rearrange("p a b -> p (a b)"), ps[:, 2 + g % 2, :], scale,
                                             biases[h % len(biases)][:, :, :].rearrange("p a b -> p (a b)"),
                                             ALU.mult, ALU.add).then_inc(sem("scores_read"), 1)
                    dve.wait_ge(sem("scores_read"), g + 1)
                    link(dve.tensor_reduce(small[:, 8 + k:10 + k], s[:, :, :], AX, ALU.max))
                    dve.tensor_scalar(small[:, k:k + 2], small[:, 8 + k:10 + k], -1.0, None, ALU.mult).then_inc(sem("max_ready"), 1)

                scores(0)
                for h in range(n_heads):
                    g = h0 + h
                    s, k = att_s[g % 2], 2 * (g % 2)
                    if h + 1 < n_heads:
                        scores(h + 1)
                    dve.wait_ge(sem("exp_done"), g + 1)
                    link(dve.reciprocal(small[:, 4 + k:6 + k], small[:, 4 + k:6 + k]))
                    for tt in range(2):
                        ins = dve.tensor_scalar(s[:, tt, :], s[:, tt, :], small[:, 4 + k + tt:5 + k + tt], None, ALU.mult)
                    ins.then_inc(sem("p_ready"), 1)
                    fill(fills // 2)
                    dve.wait_ge(sem("p_turned"), g + 1)
                    if g:
                        dve.wait_ge(sem("pv_done"), g)
                    dve.tensor_copy(att_pt[:, :, :].rearrange("p a b -> p (a b)"), psA).then_inc(sem("pt_copied"), 1)
                    fill(fills - fills // 2)
                    dve.wait_ge(sem("pv_done"), g + 1)
                    zz = z[:, h * dt:h * dt + dt, :].rearrange("p a b -> p (a b)") if z is not None else None
                    if z is None:
                        dve.tensor_copy(att_t[:, 0:dt * T], psB[:, 0:dt * T]).then_inc(sem("y_t"), 1)
                    else:
                        dve.tensor_tensor(att_t[:, 0:dt * T], psB[:, 0:dt * T], zz, ALU.mult).then_inc(sem("y_t"), 1)
                    low_y(y_hi[:, h * dt:h * dt + dt, :], y_lo[:, h * dt:h * dt + dt, :], att_t[:, 0:dt * T])

            def low_y(h, l, src):
                seen.need("y_hi")
                if len(h.shape) == 3:
                    h, l = h.rearrange("p a b -> p (a b)"), l.rearrange("p a b -> p (a b)")
                dve.tensor_tensor(l, src, h.bitcast(F32), ALU.subtract).then_inc(sem("y_lo"), 1)

            def pair(p, fill):
                raw = r_raw[p % 2]
                fl = lambda v: v[:, :, :].rearrange("p a b -> p (a b)")
                two = lambda v: v.rearrange("p (a b) -> p a b", b=CHUNK)
                dve.wait_ge(sem("shift_ready"), p + 1)
                wait_evacuated(dve, phases[f"B{p}"][0])
                for q in (1, 0, 2):
                    ins = dve.scalar_tensor_tensor(r_rkv[:, q, :], r_d[:, q, :], g2("b_mu_rkv", 8 * q + p),
                                                   raw[:, q, 1:T + 1], ALU.mult, ALU.add)
                ins.then_inc(sem("shift_read"), 1)
                dve.wait_ge(sem("shift_read"), p + 1)
                r, k, v = (r_rkv[:, q, :] for q in range(3))
                dve.tensor_scalar(r_kk, k, g2("b_k_k", p), None, ALU.mult).then_inc(sem("kk_ready"), 1)
                fill()
                dve.wait_ge(sem("sigmoids"), p + 1)
                for c in range(2):
                    ins = dve.tensor_tensor_scan(r_cs[:, c, 1:CHUNK + 1], ones[:], r_sg[:, c * CHUNK:(c + 1) * CHUNK],
                                                 0.0, ALU.mult, ALU.add)
                link(ins)
                mid = r_cs[:, :, CHUNK // 2]
                dve.tensor_scalar(small[:, 16:18], mid, KAPPA, None, ALU.mult)
                dve.tensor_scalar(small[:, 18:20], mid, -KAPPA, None, ALU.mult).then_inc(sem("mid_ready"), 1)
                fill()
                link(dve.tensor_scalar(r_af, r_aa, g2("b_k_a", p), one_minus_ka[:, p:p + 1], ALU.mult, ALU.add))
                link(dve.tensor_tensor(r_o2, k, r_af, ALU.mult))
                link(dve.scalar_tensor_tensor(r_rk, r, g2("b_r_k", p), r_o2, ALU.mult, ALU.mult))
                inverse_root(r_rs, 1e-12)
                link(dve.tensor_tensor(r_kk, r_kk, r_rs, ALU.mult))
                link(dve.tensor_tensor(r_aa, r_kk, r_aa, ALU.mult))
                dve.wait_ge(sem("decays"), p + 1)
                dve.scalar_tensor_tensor(two(r_at), two(r_kk), -1.0, r_e1[:, :, 0:CHUNK], ALU.mult, ALU.mult)
                dve.tensor_tensor(two(r_bt), two(r_aa), r_e2[:, :, 1:CHUNK + 1], ALU.mult).then_inc(sem("ab_ready"), 1)
                dve.tensor_tensor(two(r_kt), two(r_o2), r_e2[:, :, 1:CHUNK + 1], ALU.mult)
                dve.tensor_tensor(two(r_rt), two(r), r_e1[:, :, 1:CHUNK + 1], ALU.mult).then_inc(sem("kr_ready"), 1)
                fill(3)
                if p == 0:
                    dve.wait_ge(sem("masks_ready"), 1)
                dve.wait_ge(sem("inverse_reset"), p + 1)
                dve.wait_ge(sem("prod_abt"), p + 1)
                bank = lambda v: v.rearrange("p (a b) -> p a b", b=P)
                dve.copy_predicated(one_of_pair(r_xt, 0, 1), level_mask(m_level_t[0], 0), one_of_pair(bank(psA), 0, 1)).then_inc(sem("abt_read"), 1)
                dve.wait_ge(sem("prod_ab"), p + 1)
                dve.copy_predicated(one_of_pair(r_x, 0, 0), level_mask(m_level[0], 0), one_of_pair(bank(psD), 0, 0))
                dve.copy_predicated(r_cm[:, :, :], mask4(m_strict), bank(psD)).then_inc(sem("ab_read"), 1)
                dve.wait_ge(sem("prod_ak"), p + 1)
                dve.copy_predicated(r_ak[:, :, :], mask4(m_strict_t), bank(psC)).then_inc(sem("ak_read"), 1)
                dve.wait_ge(sem("prod_rb"), p + 1)
                dve.copy_predicated(r_arb[:, :, :], mask4(m_incl_t), bank(psA)).then_inc(sem("rb_read"), 1)
                for l in range(1, LEVELS):
                    n = p * (LEVELS - 1) + l
                    fill()
                    dve.wait_ge(sem("xg_done"), n)
                    ins = dve.copy_predicated(one_of_pair(r_xt, l, 1), level_mask(m_level_t[l], l), packed(psC, l))
                    if l < LEVELS - 1:
                        ins = dve.copy_predicated(one_of_pair(r_x, l, 0), level_mask(m_level[l], l), packed(psD, l))
                    ins.then_inc(sem("x_ready"), 1)
                    if l == 1:
                        dve.wait_ge(sem("prod_rk"), p + 1)
                        dve.copy_predicated(r_ark[:, :, :], mask4(m_incl_t), bank(psA)).then_inc(sem("rk_read"), 1)
                    if l == 2:
                        dve.wait_ge(sem("vbk_turned"), p + 1)
                        dve.tensor_copy(fl(r_vbk), psA).then_inc(sem("vbk_ready"), 1)
                for c in range(2):
                    dve.wait_ge(sem("w_done"), 2 * p + c + 1)
                    dve.tensor_copy(r_w[:, 0:P], psA[:, 0:P]).then_inc(sem("w_read"), 1)
                    if c == 0:
                        fill()
                    dve.wait_ge(sem("u_done"), 2 * p + c + 1)
                    dve.tensor_copy(r_u[:, c * P:(c + 1) * P], psA[:, P:2 * P]).then_inc(sem("u_read"), 1)
                    if c == 0:
                        dve.wait_ge(sem("s_done"), p + 1)
                        dve.tensor_scalar(r_s, psD[:, 0:64], r_e1[:, 0, CHUNK:CHUNK + 1], r_e2[:, 1, 0:1], ALU.mult, ALU.mult)\
                            .then_inc(sem("s_read"), 1)
                fill()
                dve.wait_ge(sem("mean_done"), p + 1)
                dve.scalar_tensor_tensor(r_dd, psC[:, 0:T], -1.0 / 64, r_o, ALU.mult, ALU.add).then_inc(sem("dev_ready"), 1)
                dve.wait_ge(sem("bonus_done"), p + 1)
                dve.wait_ge(sem("dev_ready"), p + 1)
                dve.tensor_tensor(r_kk, psD[:, 0:T], v, ALU.mult)
                fill()
                inverse_root(r_aa)
                link(dve.tensor_tensor(r_dd, r_dd, r_aa, ALU.mult))
                link(dve.tensor_scalar(r_dd, r_dd, g2("b_ln_w", p), g2("b_ln_b", p), ALU.mult, ALU.add))
                link(dve.tensor_tensor(r_dd, r_dd, r_kk, ALU.add))
                dve.tensor_tensor(r_t, r_dd, raw[:, 3, 1:T + 1], ALU.mult).then_inc(sem("rwkv_t"), 1)
                fill()
                low_y(y_hi[:, p, :], y_lo[:, p, :], r_t)

            for n in range(LEAD):
                lo(n)
            dve.wait_ge(sem("vec_turned"), 1)
            dve.tensor_copy(vec1[:, 0:n_rows1], psC[:, 0:n_rows1])
            link(dve.tensor_copy(vec2[:, 0:n_rows2], psC[:, P:P + n_rows2]))
            dve.tensor_scalar(one_minus_ka[:], vec2[:, v2["b_k_a"]:v2["b_k_a"] + 8], -1.0, 1.0, ALU.mult, ALU.add)\
                .then_inc(sem("vec_ready"), 1)
            dve.wait_ge(sem("vec_ready"), 1)
            turn([x_t[:, 2 * g:2 * g + 2, :].rearrange("p a b -> p (a b)") for g in range(8)])
            norm("norm_g")
            fill = filler(unit, ["lora", "B0"])
            fill(4)
            wait_evacuated(dve, 0)
            dve.wait_ge(sem("zeros_ready"), 1)
            link(dve.tensor_tensor(lora_x, lora[:, 0:T], lora[:, 1:T + 1], ALU.subtract))
            dve.scalar_tensor_tensor(lora_x, lora_x, g2("b_mu_w"), lora[:, 1:T + 1], ALU.mult, ALU.add).then_inc(sem("lora_shifted"), 1)
            fill.drain()
            for p in range(KB):
                fill = filler(unit, ([f"B{p + 1}"] if p + 1 < KB else []) + [f"A{p}"])
                pair(p, fill)
                fill.drain()
            values = lambda v: [v[:, tt, 512 * g:512 * g + 512] for tt in range(2) for g in range(2)]
            fill = filler(unit, ["gate_b"])
            heads_norm(a_q, "a_q_g", 1, hn_rs)
            fill(4)
            heads_norm(a_k, "a_k_g", 1, hn_rs)
            fill(4)
            turn(values(att_v))
            fill.drain()
            fill = filler(unit, ["C"])
            wait_evacuated(dve, phases["C"][0] - 1)
            attention("a", 8, 1, a_bias, a_z, fill, 4)
            fill.drain()
            run(dve, unit, "gate_a")
            run(dve, unit, "gate_c")
            dve.wait_ge(sem("mem_sums"), 4)
            sums = small[:, 20:24].rearrange("p (a b) -> p a b", b=2)
            dve.tensor_tensor(small[:, 28:30], sums[:, :, 0], sums[:, :, 1], ALU.add).then_inc(sem("mem_mean"), 1)
            inverse_root(small[:, 28:30])
            for a in range(2):
                dve.tensor_scalar(mem_rows[a], mem_rows[a], small[:, 28 + a:29 + a], None, ALU.mult).then_inc(sem("mem_scaled"), 1)

            def mem_low(q):
                seen.need("mem_hi")
                h = h_hi[:, 4 * q:4 * q + 4, :].rearrange("p a b -> p (a b)")
                l = h_lo[:, 4 * q:4 * q + 4, :].rearrange("p a b -> p (a b)")
                dve.tensor_tensor(l, mem_t[q % 2], h.bitcast(F32), ALU.subtract).then_inc(sem("mem_lo"), 1)

            for q in range(4):
                if q >= 2:
                    dve.wait_ge(sem("mem_lo"), q - 1)
                for g in range(2):
                    seen.need("turned")
                    src = ps[:, (seen.n["turned"] - 1) % 2, :]
                    for t in range(2):
                        dst = mem_t[q % 2][:, g * 512 + t * T:g * 512 + (t + 1) * T]
                        ins = dve.tensor_scalar(dst, src[:, t * T:(t + 1) * T], g1("mem_norm_g", 4 * q + 2 * g + t), None, ALU.mult)
                    ins.then_inc(sem("turn_copied"), 1)
                if q:
                    mem_low(q - 1)
            mem_low(3)
            run(dve, unit, "mem")
            heads_norm(c_q, "c_q_g", 2, c_rs)
            heads_norm(c_k, "c_k_g", 2, c_rs)
            turn(values(c_v))
            attention("c", 4, 2, [c_bias], c_z, lambda k: None, 0)
            run(dve, unit, "up_c")

            run(dve, unit, "o")
            norm("norm1_w_2")
            run(dve, unit, "Q")
            turn(values(att_v))
            fill = filler(unit, ["L", "down"])
            attention("q", 8, 1, q_bias, None, fill, 6)
            fill.drain()
            run(dve, unit, "gate_1")
            turn(values(l_v))
            fill = filler(unit, [f"V{p}" for p in range(KB)])
            for h in range(4):
                dve.wait_ge(sem("gla_z"), h + 1)
                dve.tensor_scalar(l_t2, psA[:, 0:T], g2("gla_b_2", h), 0.0, ALU.add, ALU.min).then_inc(sem("gla_min"), 1)
                dve.wait_ge(sem("gla_min"), h + 1)
                dve.wait_ge(sem("gla_ln"), h + 1)
                link(dve.tensor_tensor(l_t2, l_t2, l_t1, ALU.subtract))
                for c in range(4):
                    ins = dve.tensor_tensor_scan(l_cs[:, 64 * c:64 * c + 64], ones[:, 0:64], l_t2[:, 64 * c:64 * c + 64],
                                                 0.0, ALU.mult, ALU.add)
                ins.then_inc(sem("gla_cs"), 1)
                fill(4)
                dve.wait_ge(sem("gla_decays"), h + 1)
                dve.scalar_tensor_tensor(l_qin, l_q[:, h, :], P ** -0.5, l_e1, ALU.mult, ALU.mult)
                dve.tensor_tensor(l_kin, l_k[:, h, :], l_e2, ALU.mult).then_inc(sem("gla_in"), 1)
                dve.wait_ge(sem("gla_a"), h + 1)
                if h == 0:
                    dve.wait_ge(sem("gla_zeros"), 1)
                dve.copy_predicated(l_at[:, :, :], mask4(m_gla, 2), psB[:, 0:T].rearrange("p (a b) -> p a b", b=P))
                dve.tensor_copy(l_kt[:, :, :].rearrange("p a b -> p (a b)"), psB[:, T:2 * T]).then_inc(sem("gla_a_read"), 1)
                for c in range(3):
                    dve.wait_ge(sem("gla_kv"), 3 * h + c + 1)
                    src = psA[:, T:2 * T] if c % 2 == 0 else psD[:, T:2 * T]
                    if c:
                        link(dve.tensor_tensor(l_t2, l_s[c - 1], src, ALU.add))
                        src = l_t2
                    dve.tensor_scalar(l_s[c], src, l_e1[:, 64 * c + 63:64 * c + 64], None, ALU.mult).then_inc(sem("gla_s"), 1)
                    if c < 2:
                        dve.wait_ge(sem("gla_s"), 3 * h + c + 1)
                fill(8)
                inverse_root(l_rs)
                for e in range(2):
                    ins = dve.scalar_tensor_tensor(l_y[:, e * T:(e + 1) * T], psC[:, e * T:(e + 1) * T],
                                                   g2("gla_norm_w_2", e), l_rs, ALU.mult, ALU.mult)
                link(ins)
                dve.tensor_tensor(l_y, l_y, l_z[:, 2 * h:2 * h + 2, :].rearrange("p a b -> p (a b)"), ALU.mult).then_inc(sem("gla_y"), 1)
                fill(4)
                low_y(y_hi[:, 2 * h:2 * h + 2, :], y_lo[:, 2 * h:2 * h + 2, :], l_y)
            fill.drain()
            run(dve, unit, "gate_2")
            for q in range(2):
                low_y(y_hi[:, 4 * q:4 * q + 4, :], y_lo[:, 4 * q:4 * q + 4, :], v_y[:, 4 * q:4 * q + 4, :].rearrange("p a b -> p (a b)"))
            run(dve, unit, "gate_3")
            for q in range(4):
                merged_low(q, 4, None, 0)
            run(dve, unit, "o2")
            norm("norm2_w_2")
            run(dve, unit, "ffn")
            run(dve, unit, "ffn_down")
            norm("final_norm_w_2", last=True)
            for a in range(2):
                for g in range(4):
                    seen.need("turned")
                    ins = dve.tensor_copy(x_rows[:, a, 512 * g:512 * g + 512], ps[:, (seen.n["turned"] - 1) % 2, :])
                    ins.then_inc(sem("turn_copied"), 1)

        @block.tensor
        def _(pe):
            seen = Seen(pe)
            operands = {"h": (h_hi, h_lo), "y": (y_hi, y_lo), "f": (f_hi, f_lo)}

            def unit(n, i=None, per=0, body=0, part=None):
                m, u = units[n]
                b, slot, s = blocks[m], n % RING, m % 2
                k_tiles, tiles = KINDS[b.kind]
                x_hi, x_lo = operands[b.operand]
                if part != 1:
                    if u == 0 and m >= 2:
                        wait_evacuated(pe, m - 2, i, body)
                    pe.wait_ge(sem("lo_done"), on(i, n + 1, per))
                    if m in operand_ready:
                        name, before, size = operand_ready[m]
                        pe.wait_ge(sem(name), before + (u * k_tiles + k_tiles - 1) // size + 1)
                last_k = b.kt - 1
                half = k_tiles // 2
                for j in {None: range(k_tiles), 0: range(half), 1: range(half, k_tiles)}[part]:
                    k = u * k_tiles + j
                    for c in range(tiles):
                        o = gp[:, s, c * T:(c + 1) * T]
                        at = (j * tiles + c) * P
                        wh, wl = w_hi[:, slot, at:at + P], w_lo[:, slot, at:at + P]
                        pe.matmul(o, wh, x_hi[:, k, :], start=(k == 0 and c % 2 == 0), stop=False, skip_group_check=True)
                        pe.matmul(o, wh, x_lo[:, k, :], start=False, stop=False, skip_group_check=True)
                        ins = pe.matmul(o, wl, x_hi[:, k, :], start=False, stop=(k == last_k), skip_group_check=True)
                if part != 0:
                    ins.then_inc(sem("unit_used"), 1)

            def fill_halves(names):
                todo = [(n, part) for name in names for n in range(first[phases[name][0]], last_unit(phases[name][0] + phases[name][1] * phases[name][2] - 1) + 1)
                        for part in range(2)]

                def fill(k=1):
                    for _ in range(int(2 * k)):
                        if todo:
                            n, part = todo.pop(0)
                            unit(n, part=part)
                fill.drain = lambda: fill(len(todo))
                return fill

            operand_ready = {
                phases["lora"][0]: ("norm_lo", 0, 4),
                phases["mem"][0]: ("mem_lo", 0, 4),
                phases["up_c"][0]: ("y_lo", KB + 8, 2),
                phases["o"][0]: ("merged_lo", 0, 4),
                phases["Q"][0]: ("norm_lo", 4, 4),
                phases["o2"][0]: ("merged_lo", 4, 4),
                phases["ffn"][0]: ("norm_lo", 8, 4),
                phases["gate_3"][0] + 1: ("y_lo", KB + 24, 4)}

            def turn(batches):
                for tiles in batches:
                    if pe_n["turn"] >= 2:
                        pe.wait_ge(sem("turn_copied"), pe_n["turn"] - 1)
                    bank = ps[:, pe_n["turn"] % 2, :]
                    for j, src in enumerate(tiles):
                        ins = pe.transpose(bank[:, j * P:(j + 1) * P], src, ident[:])
                    ins.then_inc(sem("turned"), 1)
                    pe_n["turn"] += 1

            pe_n = Counter()

            def norm():
                for q in range(4):
                    seen.need("norm_sq")
                    for t in range(4):
                        ins = pe.matmul(psC[:, 0:T], ones[:], n_sq[q % 2][:, t * T:(t + 1) * T],
                                        start=(q == 0 and t == 0), stop=(q == 3 and t == 3))
                    ins.then_inc(sem("norm_sq_used"), 1)

            def heads_norm(per_head, buf):
                for _ in range(2):
                    seen.need("hn_sq")
                    if pe_n["hn"]:
                        pe.wait_ge(sem("hn_done"), pe_n["hn"])
                    pe_n["hn"] += 1
                    for t in range(4):
                        hd = t // per_head
                        ins = pe.matmul(psCD[:, hd * T:(hd + 1) * T], ones[:], buf[:, t * T:(t + 1) * T],
                                        start=(t % per_head == 0), stop=(t % per_head == per_head - 1))
                    ins.then_inc(sem("hn_sq_used"), 1)

            def attention(which, n_heads, dt, q, k, v, fill, fills):
                h0 = HEAD0[which]

                def scores(h):
                    g = h0 + h
                    if g >= 2:
                        pe.wait_ge(sem("scores_read"), g - 1)
                    for tt in range(2):
                        for d in range(dt):
                            ins = pe.matmul(ps[:, 2 + g % 2, tt * T:(tt + 1) * T], q[:, h * dt + d, tt * P:(tt + 1) * P],
                                            k[:, h * dt + d, :], start=(d == 0), stop=(d == dt - 1))
                    ins.then_inc(sem("scores_done"), 1)

                scores(0)
                for h in range(n_heads):
                    g = h0 + h
                    if h + 1 < n_heads:
                        scores(h + 1)
                    fill(fills // 2)
                    pe.wait_ge(sem("p_ready"), g + 1)
                    if g:
                        pe.wait_ge(sem("pt_copied"), g)
                    for tt in range(2):
                        for kt in range(2):
                            ins = pe.transpose(psA[:, kt * T + tt * P:kt * T + (tt + 1) * P],
                                               att_s[g % 2][:, tt, kt * P:(kt + 1) * P], ident[:])
                    ins.then_inc(sem("p_turned"), 1)
                    fill(fills - fills // 2)
                    pe.wait_ge(sem("pt_copied"), g + 1)
                    if h:
                        pe.wait_ge(sem("y_t"), y_before[which] + h)
                    for d in range(dt):
                        for kt in range(2):
                            at = (h * dt + d) * P
                            ins = pe.matmul(psB[:, d * T:(d + 1) * T], v[:, kt, at:at + P], att_pt[:, kt, :],
                                            start=(kt == 0), stop=(kt == 1))
                    ins.then_inc(sem("pv_done"), 1)

            y_before = HEAD0

            def pair(p, fill):
                four = [(hh, c) for hh in range(2) for c in range(2)]

                def rows(hh):
                    return slice(64 * hh, 64 * hh + 64)

                def settle(ins):
                    ins.then_inc(sem("rows_done"), 1)
                    seen.need("rows_done")

                def products(bank, left, right, name):
                    for n, (hh, c) in enumerate(four):
                        if n == 2:
                            settle(ins)
                        ins = pe.matmul(bank[:, n * P:(n + 1) * P], left[rows(hh), c * P:(c + 1) * P],
                                        right[rows(hh), c * P:(c + 1) * P], start=True, stop=True)
                    ins.then_inc(sem(name), 1)

                cols = slice(p * P, (p + 1) * P)
                if p:
                    pe.wait_ge(sem("y_lo"), p)
                settle(pe.matmul(psA[:, 0:T], w2a2[0:64, cols], lora_x[0:64, :], start=True, stop=True))
                pe.matmul(psA[:, T:2 * T], w2a2[64:128, cols], lora_x[64:128, :], start=True, stop=True).then_inc(sem("lora_z"), 1)
                fill()
                pe.wait_ge(sem("kk_sq"), p + 1)
                pe.matmul(psB[:, 0:T], blk[:], r_sq, start=True, stop=True).then_inc(sem("kk_sum"), 1)
                fill(3)
                pe.wait_ge(sem("ab_ready"), p + 1)
                products(psA, r_bt, r_at, "prod_abt")
                products(psD, r_at, r_bt, "prod_ab")
                pe.wait_ge(sem("kr_ready"), p + 1)
                products(psC, r_kt, r_at, "prod_ak")
                fill()
                pe.wait_ge(sem("abt_read"), p + 1)
                products(psA, r_bt, r_rt, "prod_rb")
                fl = lambda v, n: v[:, n, :]
                for l in range(1, LEVELS):
                    n = p * (LEVELS - 1) + l
                    if l == 1:
                        pe.wait_ge(sem("ab_read"), p + 1)
                    else:
                        pe.wait_ge(sem("x_ready"), n - 1)
                    for t in range(4):
                        ins = pe.matmul(packed(psB, l)[:, t], r_cm[:, t, :], one_of_pair(r_xt, l, 1)[:, t], start=True, stop=True)
                    ins.then_inc(sem("g_done"), 1)
                    if l == 1:
                        pe.wait_ge(sem("rb_read"), p + 1)
                        products(psA, r_kt, r_rt, "prod_rk")
                    if l == 2:
                        pe.wait_ge(sem("rk_read"), p + 1)
                        for t, src in enumerate((r_rkv[:, 2, 0:P], r_rkv[:, 2, P:T], r_bt[:, 0:P], r_kt[:, 0:P])):
                            ins = pe.transpose(psA[:, t * P:(t + 1) * P], src, ident[:])
                        ins.then_inc(sem("vbk_turned"), 1)
                    fill(0.5)
                    pe.wait_ge(sem("g_read"), n)
                    if l == 1:
                        pe.wait_ge(sem("ak_read"), p + 1)
                    for t in range(4):
                        ins = pe.matmul(packed(psC, l)[:, t], r_x[:, t, :], one_of_pair(r_g, l, 1)[:, t], start=True, stop=True)
                    if l < LEVELS - 1:
                        for t in range(4):
                            ins = pe.matmul(packed(psD, l)[:, t], r_g[:, t, :], one_of_pair(r_x, l, 0)[:, t], start=True, stop=True)
                    ins.then_inc(sem("xg_done"), 1)
                    fill(0.5)
                pe.wait_ge(sem("vbk_ready"), p + 1)
                for c in range(2):
                    vc = r_vbk[:, c, :]
                    if c:
                        pe.wait_ge(sem("s_read"), p + 1)
                    for hh in range(2):
                        o = psA[:, hh * 64:hh * 64 + 64]
                        if c:
                            settle(pe.matmul(o, r_at[rows(hh), P:T], r_s[rows(hh), :], start=True, stop=False))
                        ins = pe.matmul(o, r_ak[:, 2 * hh + c, :], vc[:, rows(hh)], start=not c, stop=True)
                    ins.then_inc(sem("w_done"), 1)
                    if c == 0:
                        fill(0.5)
                    pe.wait_ge(sem("w_read"), 2 * p + c + 1)
                    if c == 0:
                        pe.wait_ge(sem("x_ready"), (p + 1) * (LEVELS - 1))
                    for hh in range(2):
                        ins = pe.matmul(psA[:, P + hh * 64:P + hh * 64 + 64], r_xt[:, 2 * hh + c, :],
                                        r_w[:, hh * 64:hh * 64 + 64], start=True, stop=True)
                    ins.then_inc(sem("u_done"), 1)
                    if c == 0:
                        fill(0.5)
                    pe.wait_ge(sem("u_read"), 2 * p + c + 1)
                    uc = r_u[:, c * P:(c + 1) * P]
                    if c == 0:
                        for hh in range(2):
                            o = psD[rows(hh), 0:64]
                            pe.matmul(o, r_vbk[:, 2, rows(hh)], uc[:, rows(hh)], start=True, stop=False)
                            ins = pe.matmul(o, r_vbk[:, 3, rows(hh)], vc[:, rows(hh)], start=False, stop=True)
                        ins.then_inc(sem("s_done"), 1)
                    for hh in range(2):
                        o = psB[rows(hh), c * P:(c + 1) * P]
                        pe.matmul(o, vc[:, rows(hh)], r_ark[:, 2 * hh + c, :], start=True, stop=False)
                        ins = pe.matmul(o, uc[:, rows(hh)], r_arb[:, 2 * hh + c, :], start=False, stop=not c)
                        if c:
                            ins = pe.matmul(o, r_s[rows(hh), :], r_rt[rows(hh), P:T], start=False, stop=True)
                ins.then_inc(sem("o_done"), 1)
                fill()
                pe.wait_ge(sem("o_read"), p + 1)
                pe.matmul(psC[:, 0:T], blk[:], r_o, start=True, stop=True).then_inc(sem("mean_done"), 1)
                pe.matmul(psD[:, 0:T], blk[:], r_rk, start=True, stop=True).then_inc(sem("bonus_done"), 1)
                fill()
                pe.wait_ge(sem("dev_sq"), p + 1)
                pe.matmul(psC[:, T:2 * T], blk[:], r_sq, start=True, stop=True).then_inc(sem("var_done"), 1)
                fill(2)

            pe.wait_ge(sem("ident_ready"), 1)
            pe.wait_ge(sem("rows_landed"), 16 * N_ROW_DMAS)
            pe.transpose(psC[:, 0:n_rows1], rows1[0:n_rows1, :], ident[0:n_rows1, 0:n_rows1])
            pe.transpose(psC[:, P:P + n_rows2], rows2[0:n_rows2, :], ident[0:n_rows2, 0:n_rows2]).then_inc(sem("vec_turned"), 1)
            pe.wait_ge(sem("ones_ready"), 1)
            for a in range(2):
                pe.wait_ge(sem(f"x_landed{a}"), 16)
            turn([[x_rows[:, a, t * P:(t + 1) * P] for t in (2 * g, 2 * g + 1) for a in range(2)] for g in range(8)])
            pe.wait_ge(sem("vec_ready"), 1)
            norm()
            fill = filler(unit, ["lora", "B0"])
            fill.drain()
            pe.wait_ge(sem("lora_ready"), 1)
            pe.wait_ge(sem("w2_landed"), 32)
            for p in range(KB):
                fill = fill_halves(([f"B{p + 1}"] if p + 1 < KB else []) + [f"A{p}"])
                pair(p, fill)
                fill.drain()
            values = lambda v: [[v[:, 4 * g + t, tt * P:(tt + 1) * P] for t in range(4)] for tt in range(2) for g in range(2)]
            pe.wait_ge(sem("y_lo"), KB)
            fill = filler(unit, ["gate_b"])
            heads_norm(1, hn_sq)
            fill(4)
            heads_norm(1, hn_sq)
            fill(4)
            turn(values(a_vraw))
            fill.drain()
            fill = filler(unit, ["C"])
            pe.wait_ge(sem("hn_done"), 4)
            pe.wait_ge(sem("turn_copied"), pe_n["turn"])
            attention("a", 8, 1, a_q, a_k, att_v, fill, 4)
            fill.drain()
            pe.wait_ge(sem("y_lo"), HEAD0["a"] + 8 + KB)
            run(pe, unit, "gate_a")
            run(pe, unit, "gate_c")
            pe.wait_ge(sem("mem_scaled"), 2)
            turn([[mem_rows[a][:, t * P:(t + 1) * P] for t in (2 * g, 2 * g + 1) for a in range(2)] for g in range(8)])
            run(pe, unit, "mem")
            heads_norm(2, c_sq)
            heads_norm(2, c_sq)
            wait_evacuated(pe, phases["up_c"][0] - 1)
            wait_evacuated(pe, phases["up_c"][0] - 2)
            turn(values(c_vraw))
            pe.wait_ge(sem("hn_done"), 8)
            pe.wait_ge(sem("turn_copied"), pe_n["turn"])
            attention("c", 4, 2, c_q, c_k, c_v, lambda k: None, 0)
            run(pe, unit, "up_c")
            run(pe, unit, "o")
            norm()
            run(pe, unit, "Q")
            wait_evacuated(pe, phases["L"][0] - 1)
            wait_evacuated(pe, phases["L"][0] - 2)
            turn(values(q_vraw))
            pe.wait_ge(sem("turn_copied"), pe_n["turn"])
            fill = filler(unit, ["L", "down"])
            attention("q", 8, 1, q_q, q_k, att_v, fill, 6)
            fill.drain()
            pe.wait_ge(sem("y_lo"), KB + 20)
            run(pe, unit, "gate_1")
            turn(values(l_vraw))
            fill = filler(unit, [f"V{p}" for p in range(KB)])
            pe.wait_ge(sem("up_landed"), 16)
            pe.wait_ge(sem("turn_copied"), pe_n["turn"])
            for h in range(4):
                if h:
                    pe.wait_ge(sem("gla_y"), h)
                pe.matmul(psA[:, 0:T], l_up[0:16, h * P:(h + 1) * P], l_down[0:16, :], start=True, stop=True).then_inc(sem("gla_z"), 1)
                fill(4)
                pe.wait_ge(sem("gla_in"), h + 1)
                for tt in range(2):
                    pe.matmul(psB[:, tt * P:(tt + 1) * P], l_kin[:, tt * P:(tt + 1) * P], l_qin[:, tt * P:(tt + 1) * P],
                              start=True, stop=True)
                for tt in range(2):
                    ins = pe.transpose(psB[:, T + tt * P:T + (tt + 1) * P], l_kin[:, tt * P:(tt + 1) * P], ident[:])
                ins.then_inc(sem("gla_a"), 1)
                pe.wait_ge(sem("gla_a_read"), h + 1)
                for c in range(3):
                    half = slice(64 * (c % 2), 64 * (c % 2) + 64)
                    if c == 2:
                        pe.wait_ge(sem("gla_s"), 3 * h + 1)
                    pe.matmul((psA if c % 2 == 0 else psD)[:, T:2 * T], l_kt[half, c // 2, :], l_v[half, c // 2, h * T:(h + 1) * T],
                              start=True, stop=True).then_inc(sem("gla_kv"), 1)
                for e in range(2):
                    for tt in range(2):
                        at = h * T + e * P
                        pe.matmul(psC[:, e * T + tt * P:e * T + (tt + 1) * P], l_v[:, tt, at:at + P], l_at[:, tt, :],
                                  start=(e == 0 and tt == 0), stop=(tt == 0), skip_group_check=True)
                fill(4)
                pe.wait_ge(sem("gla_s"), 3 * h + 3)
                for e in range(2):
                    for c in range(1, 4):
                        ins = pe.matmul(psC[:, e * T + 64 * c:e * T + 64 * c + 64], l_s[c - 1][:, e * P:(e + 1) * P],
                                        l_qin[:, 64 * c:64 * c + 64], start=False, stop=True, skip_group_check=True)
                ins.then_inc(sem("gla_o"), 1)
                fill(4)
                pe.wait_ge(sem("gla_sq"), h + 1)
                for e in range(2):
                    ins = pe.matmul(psD[:, 0:T], ones[:], l_sq[:, e, :], start=(e == 0), stop=(e == 1))
                ins.then_inc(sem("gla_ss"), 1)
                fill(4)
            fill.drain()
            pe.wait_ge(sem("y_lo"), KB + 24)
            run(pe, unit, "gate_2")
            run(pe, unit, "gate_3")
            run(pe, unit, "o2")
            norm()
            run(pe, unit, "ffn")
            wait_evacuated(pe, phases["ffn_down"][0] - 1)
            run(pe, unit, "ffn_down")
            norm()
            pe.wait_ge(sem("norm_t"), 16)
            turn([[x_t[:, 4 * g + t, a * P:(a + 1) * P] for t in range(4)] for a in range(2) for g in range(4)])


def kernel(**inputs):
    from concourse import bacc
    from concourse.bass_utils import run_bass_kernel_spmd

    nc = bacc.Bacc("TRN2", target_bir_lowering=False, num_devices=1)
    arrays, dram = {}, {}
    for name, a in inputs.items():
        a = np.ascontiguousarray(a)
        arrays[f"in_{name}"] = a
        dram[name] = nc.dram_tensor(f"in_{name}", a.shape, mybir.dt.from_np(a.dtype), kind="ExternalInput").ap()
    out = nc.dram_tensor("out_x", (1, T, D), F32, kind="ExternalOutput").ap()
    build(nc, dram, out)
    r = run_bass_kernel_spmd(nc, [arrays], core_ids=[0])
    return r.results[0]["out_x"]
```

```python
from collections import Counter, namedtuple
from contextlib import ExitStack

import numpy as np

import concourse.bass as bass
from concourse import mybir

ALU = mybir.AluOpType
ACT = mybir.ActivationFunctionType
F32 = mybir.dt.float32
F32R = mybir.dt.float32r
U8 = mybir.dt.uint8
AX = mybir.AxisListType.X

P = 128
T = 256
D = 2048
KD = D // P
BW = 1024
KB = BW // P
CHUNK = 128
FF = 5632
KF = FF // P
UNIT = 1024
RING = 4
LEAD = 3
EPS = 1e-6
GN_EPS = 64e-5
KAPPA = float(np.exp(-0.5))
MASKED = -1e30
LEVELS = 7

A_COL, B_COL, LORA_COL, C_COL = 0, 4096, 8192, 8320
GA_COL, GB_COL, GC_COL = 10368, 12416, 14464
Q_COL, L_COL, DOWN_COL, V_COL, M_COL = 0, 3072, 6144, 6160, 9232

Block = namedtuple("Block", "weight kt kind base col step operand evac arg")
KINDS = {"wide": (2, 4), "pair": (2, 4), "trio": (2, 3), "narrow": (4, 1)}

DMAS = {"wide": 1, "pair": 2, "trio": 2, "narrow": 1}


def plan_stream():
    blocks, phases = [], {}

    def phase(name, body, bodies=1):
        phases[name] = (len(blocks), len(body), bodies)
        for i in range(bodies):
            blocks.extend(b._replace(col=b.col + i * b.step, arg=b.arg + i * len(body)) for b in body)

    def wide(w, col, n, step, operand, evac, kt=KD):
        return [Block(w, kt, "wide", 0, col + 512 * j, step, operand, evac, j) for j in range(n)]

    def gated(w, gate_col, up, evac):
        return [b for j in range(2) for b in (
            Block(w, KD, "wide", 0, gate_col + 512 * j, 1024, "h", "gate", 2 * j),
            Block(up, KB, "wide", 0, 512 * j, 1024, "y", evac, 2 * j + 1))]

    phase("lora", [Block("w_in", KD, "narrow", 0, LORA_COL, 0, "h", "lora", 0)])
    for p in range(-1, KB):
        if p + 1 < KB:
            phase(f"B{p + 1}", [Block("w_in", KD, "pair", B_COL, P * (p + 1), 0, "h", "rwkv", p + 1)])
        if p >= 0:
            phase(f"A{p}", [Block("w_in", KD, "wide", 0, A_COL + 512 * p, 0, "h", "a_cols", p)])
    gate_b = [b._replace(col=b.col + i * b.step, arg=b.arg + 4 * i) for i in range(2) for b in gated("w_in", GB_COL, "w_up_b", "merge0")]
    phase("gate_b0", gate_b[:1])
    phase("gate_b", gate_b[1:])
    phase("C", wide("w_in", C_COL, 4, 0, "h", "c_cols"))
    phase("gate_a", gated("w_in", GA_COL, "w_up_a", "merge"), 2)
    phase("mem", wide("w_mem_kv", 0, 2, 1024, "mem", "mem"), 2)
    phase("gate_c", wide("w_in", GC_COL, 2, 1024, "h", "gate_c"), 2)
    phase("up_c", wide("w_up_c", 0, 2, 1024, "y", "merge_c", KB), 2)
    phase("o", wide("w_o", 0, 2, 1024, "h", "residual"), 2)
    phase("Q", wide("w_in_2", Q_COL, 2, 1024, "h", "q_cols"), 3)
    phase("L", wide("w_in_2", L_COL, 6, 0, "h", "l_cols"))
    phase("down", [Block("w_in_2", KD, "narrow", 0, DOWN_COL, 0, "h", "gla_down", 0)])
    phase("gate_1", gated("w_in_2", M_COL, "w_br_attn_2", "merge0"), 2)
    for p in range(KB):
        phase(f"V{p}", [Block("w_in_2", KD, "trio", V_COL, P * p, 0, "h", "conv", p)])
    phase("gate_2", gated("w_in_2", M_COL + 2048, "w_br_gla_2", "merge"), 2)
    phase("gate_3", gated("w_in_2", M_COL + 4096, "w_br_conv_2", "merge"), 2)
    phase("o2", wide("w_out_2", 0, 2, 1024, "h", "residual"), 2)
    phase("ffn", [Block("w_ffn_gate_2", KD, "wide", 0, 0, 512, "h", "ffn_gate", 0),
                  Block("w_ffn_up_2", KD, "wide", 0, 0, 512, "h", "ffn_up", 1)], 11)
    phase("ffn_down", wide("w_ffn_down_2", 0, 2, 1024, "f", "residual", KF), 2)
    units, first = [], []
    for m, b in enumerate(blocks):
        first.append(len(units))
        units.extend((m, u) for u in range(b.kt // KINDS[b.kind][0]))
    return blocks, phases, units, first


ROWS1 = [("norm_g", 16), ("mem_norm_g", 16), ("norm1_w_2", 16), ("norm2_w_2", 16), ("final_norm_w_2", 16)]
ROWS2 = [("b_mu_rkv", 24), ("b_w0", 8), ("b_a0", 8), ("b_k_k", 8), ("b_k_a", 8), ("b_r_k", 8), ("b_ln_w", 8),
         ("b_ln_b", 8), ("a_q_g", 1), ("a_k_g", 1), ("c_q_g", 2), ("c_k_g", 2), ("gla_b_2", 4), ("gla_norm_w_2", 2),
         ("conv_w_2", 24), ("b_mu_w", 1)]


N_ROW_DMAS = len(ROWS1) + len(ROWS2) + 1
HEAD0 = {"a": 0, "c": 8, "q": 12}
TURNS = {"x": 8, "a": 12, "mem": 20, "c": 24, "q": 28, "l": 32, "out": 40}


def build(nc, dram, out):
    blocks, phases, units, first = plan_stream()
    n_units = len(units)
    landed = []
    for n, (m, _) in enumerate(units):
        landed.append((landed[n - RING] if n >= RING else 0) + 16 * DMAS[blocks[m].kind])

    def last_unit(m):
        return first[m + 1] - 1 if m + 1 < len(first) else n_units - 1

    with ExitStack() as ctx:
        sem_of = {}

        def sem(name):
            if name not in sem_of:
                sem_of[name] = ctx.enter_context(nc.semaphore(name))
            return sem_of[name]

        def sb(name, shape, dt=F32, where=ctx):
            return where.enter_context(nc.sbuf_tensor(name, shape, dt))

        w_raw = sb("w_raw", [P, RING, UNIT])
        w_hi = sb("w_hi", [P, RING, UNIT], F32R)
        w_lo = sb("w_lo", [P, RING, UNIT], F32R)
        x_t = sb("x_t", [P, KD, T])
        h_hi = sb("h_hi", [P, KD, T], F32R)
        h_lo = sb("h_lo", [P, KD, T], F32R)
        ident = sb("ident", [P, P])
        ones = sb("ones", [P, P])
        blk = sb("blk", [P, P])
        m_strict = sb("m_strict", [P, P], U8)
        m_incl_t = sb("m_incl_t", [P, P], U8)
        m_strict_t = sb("m_strict_t", [P, P], U8)
        m_gla = sb("m_gla", [P, P], U8)
        m_level = [sb(f"m_level{l}", [P, P // 2], U8) for l in range(LEVELS)]
        m_level_t = [sb(f"m_level_t{l}", [P, P // 2], U8) for l in range(LEVELS)]
        m_work = sb("m_work", [P, P])
        vec1 = sb("vec1", [P, 80])
        vec2 = sb("vec2", [P, 128])
        one_minus_ka = sb("one_minus_ka", [P, KB])
        small = sb("small", [P, 32])
        last_sq = [sb("last_sq", [P, UNIT])[:]]
        y_ctx = ExitStack()
        y_hi = sb("y_hi", [P, KB, T], F32R, y_ctx)
        y_lo = sb("y_lo", [P, KB, T], F32R, y_ctx)
        ARENA = 83 * 256
        with ExitStack() as mem_ctx:
            mem_lo = sb("mem_lo", [P, KD, T], F32R, mem_ctx)
        arena = sb("arena", [P, ARENA], F32, y_ctx)
        y_ctx.close()
        f_hi = sb("f_hi", [P, KF, T], F32R)
        f_lo = sb("f_lo", [P, KF, T], F32R)
        f_t = sb("f_t", [P, 2, UNIT])
        rel = nc.dram_tensor("rel_scratch", (8, 384), F32, kind="Internal")

        def unit_size(n):
            k, tiles = KINDS[blocks[units[n][0]].kind]
            return k * tiles * P

        def area(kb, *shape):
            at, size = int(kb * 256), int(np.prod(shape))
            assert at + size <= ARENA, (kb, shape)
            v = arena[:, at:at + size]
            if len(shape) == 2:
                v = v.rearrange("p (a b) -> p a b", b=shape[1])
            return v

        v1, v2, at = {}, {}, 0
        for name, rows in ROWS1:
            v1[name], at = at, at + rows
        n_rows1, at = at, 0
        for name, rows in ROWS2:
            v2[name], at = at, at + rows
        n_rows2 = at

        def g1(name, t=0):
            return vec1[:, v1[name] + t:v1[name] + t + 1]

        def g2(name, t=0):
            return vec2[:, v2[name] + t:v2[name] + t + 1]

        gp = ctx.enter_context(nc.psum_tensor("gp", [P, 2, UNIT], F32))
        ps = ctx.enter_context(nc.psum_tensor("ps", [P, 4, 512], F32))
        psA, psB, psC, psD = (ps[:, b, :] for b in range(4))
        psCD = ps[:, 2:4, :].rearrange("p a b -> p (a b)")

        x_rows = area(0, 2, D)
        rows1, rows2 = area(16, P), area(16.5, P)
        n_sq = [area(64, UNIT), area(68, UNIT)]
        a_q, a_k, a_vraw, a_z = area(0, KB, T), area(8, KB, T), area(16, KB, T), area(24, KB, T)
        r_raw = [area(32, 4, T + 1), area(36.25, 4, T + 1)]
        lora, lora_x, w2a2 = area(40.5, T + 1), area(41.75, T), area(42.75, BW)
        r_d, r_rkv = area(46.75, 3, T), area(49.75, 3, T)
        r_sg, r_aa, r_kk, r_sq, r_rs = (area(52.75 + j, T) for j in range(5))
        r_cs, r_e1, r_e2 = (area(57.75 + 1.125 * j, 2, CHUNK + 1) for j in range(3))
        r_at, r_bt, r_kt, r_rt, r_rk = (area(61.25 + j, T) for j in range(5))
        r_cm, r_x, r_xt, r_g, r_ak, r_arb, r_ark, r_vbk = (area(66.25 + 2 * j, 4, P) for j in range(8))
        r_s = area(82.25, 64)
        r_w, r_u = r_sg, r_sq
        r_o, r_dd, r_t, r_o2, r_af = r_kk, r_rs, r_d[:, 0, :], r_d[:, 1, :], r_d[:, 2, :]
        mg, sig, prod = area(32, KD * T), area(48, UNIT), area(52, UNIT)
        att_v = area(56, 2, BW)
        att_s, att_pt, att_t = [area(48, 2, T), area(50, 2, T)], area(52, 2, T), area(54, 2 * T)
        a_bias, a_hankel = [area(64, 2, T), area(66, 2, T)], [area(68, T), area(69, T)]
        ext = area(70, 384)[0:8, :]
        hn_sq, hn_rs = area(64, UNIT), area(68, UNIT)
        c_q, c_z = area(72, KB, T), area(16, KB, T)
        sig_c = area(0, 4 * UNIT)
        mem_rows = [area(56, D), area(64, D)]
        mem_t = [area(24, UNIT), area(28, UNIT)]
        c_k, c_vraw, c_v = area(24, KB, T), area(56, KB, T), area(64, 2, BW)
        c_sq, c_rs = area(48, UNIT), area(52, UNIT)
        c_bias = area(80, 2, T)
        q_all = area(0, 3 * 2 * UNIT)
        q_q, q_k, q_vraw = area(0, KB, T), area(8, KB, T), area(16, KB, T)
        q_bias, q_dist = [area(32, 2, T), area(34, 2, T)], area(36, 2, T)
        l_q, l_k, l_vraw, l_z = area(24, 4, T), area(28, 4, T), area(64, KB, T), area(72, KB, T)
        l_down, l_up, l_v = area(80, T), area(81, 512), area(56, 2, BW)
        v_raw = [area(0, 3, T), area(3, 3, T)]
        v_cu, v_y, v_t = area(6, T + 2), area(8, KB, T), area(16, T)
        l_kv, l_e1, l_e2, l_qin, l_kin = area(17, T), area(20, T), area(21, T), area(22, T), area(23, T)
        l_exp, l_log, l_cs = area(68, 4 * T), area(48, 4 * T), area(52, 4 * T)
        l_at, l_kt, l_sq = area(64, 2, P), area(65, 2, P), area(66, 2, T)
        l_s = [area(68 + j, T) for j in range(3)]
        l_y = area(48, 2 * T)
        l_rs = area(50, T)

        def one_of_pair(v, l, e):
            return v[:, :, :].rearrange("p a (b e w) -> p a b e w", e=2, w=1 << l)[:, :, :, e, :]

        def packed(v, l):
            return v[:, 0:4 * P // 2].rearrange("p (a b w) -> p a b w", a=4, w=1 << l)

        def level_mask(v, l):
            return v[:].rearrange("p (b w) -> p b w", w=1 << l).unsqueeze(1).to_broadcast([P, 4, P // (2 << l), 1 << l])

        def mask4(v, n=4):
            return v[:].unsqueeze(1).to_broadcast([P, n, P])

        block = ctx.enter_context(nc.Block())

        class Seen:

            def __init__(self, eng):
                self.eng, self.n = eng, Counter()

            def need(self, name, k=1):
                self.n[name] += k
                self.eng.wait_ge(sem(name), self.n[name])

            def skip(self, name, k=1):
                self.n[name] += k

        def on(i, const, each):
            return const if i is None else i * each + const

        def wait_evacuated(eng, m, i=None, body=0):
            eng.wait_ge(sem(f"evacuated{m % 2}"), on(i, m // 2 + 1, body // 2))

        def run(eng, unit, name, straight=()):
            m0, body, bodies = phases[name]
            n0 = first[m0]
            per = (first[m0 + body] if m0 + body < len(first) else n_units) - n0
            loops = bodies > 1 and name not in straight and name not in ("mem", "gate_1", "ffn_down", list(phases)[-1])
            if not loops:
                for n in range(n0, n0 + per * bodies):
                    unit(n)
                return
            with eng.Fori(0, bodies) as i:
                for n in range(n0, n0 + per):
                    unit(n, i, per, body)

        def filler(unit, names):
            todo = [n for name in names for n in range(first[phases[name][0]], last_unit(phases[name][0] + phases[name][1] * phases[name][2] - 1) + 1)]

            def fill(k=1):
                for _ in range(k):
                    if todo:
                        unit(todo.pop(0))
            fill.drain = lambda: fill(len(todo))
            return fill

        def source(b, u, col):
            per = KINDS[b.kind][0]
            w = dram[b.weight].rearrange("l (k p) n -> (l k) p n", p=P).rearrange("k p n -> p k n")
            w = w[:, per * u:per * u + per, :]
            if b.kind == "narrow":
                return w[:, :, b.col:b.col + 128]
            if b.kind == "wide":
                return w[:, :, bass.ds(col, 512)]
            q = KINDS[b.kind][1]
            return w[:, :, b.base:b.base + 1024 * q].rearrange("p k (q c) -> p k q c", q=q)[:, :, :, b.col:b.col + P]

        @block.sync
        def _(sp):
            x_in = dram["x"].rearrange("b (a p) d -> (b a) p d", p=P)
            for a in range(2):
                sp.dma_start(x_rows[:, a, :], x_in[a]).then_inc(sem(f"x_landed{a}"), 16)
            for name, rows in ROWS1:
                src = dram[name]
                src = src.rearrange("l (r c) -> (l r) c", c=P) if len(src.shape) == 2 else src.rearrange("(r c) -> r c", c=P)
                sp.dma_start(rows1[v1[name]:v1[name] + rows, :], src).then_inc(sem("rows_landed"), 16)
            n_dma = len(ROWS1)
            for name, rows in ROWS2:
                at = v2[name]
                if name == "b_mu_w":
                    sp.dma_start(rows2[at:at + 1, 0:64], dram["b_mu_w"]).then_inc(sem("rows_landed"), 16)
                    sp.dma_start(rows2[at:at + 1, 64:128], dram["b_mu_a"]).then_inc(sem("rows_landed"), 16)
                    n_dma += 2
                    continue
                src = dram[name]
                if name == "b_r_k":
                    src = src.rearrange("l h d -> l (h d)")
                src = src.rearrange("l k (r c) -> (l k r) c", c=P) if len(src.shape) == 3 else src.rearrange("l (r c) -> (l r) c", c=P)
                sp.dma_start(rows2[at:at + rows, :], src).then_inc(sem("rows_landed"), 16)
                n_dma += 1
            assert n_dma == N_ROW_DMAS

            def unit(n, i=None, per=0, body=0):
                m, u = units[n]
                b, slot = blocks[m], n % RING
                col = b.col if i is None else i * b.step + b.col
                if n >= RING:
                    sp.wait_ge(sem("lo_done"), on(i, n - RING + 1, per))
                k, tiles = KINDS[b.kind]
                dst = w_raw[:, slot, 0:k * tiles * P].rearrange("p (k n) -> p k n", k=k)
                if DMAS[b.kind] == 1:
                    sp.dma_start(dst, source(b, u, col)).then_inc(sem(f"landed{slot}"), 16)
                    return
                for j in range(k):
                    sp.dma_start(dst[:, j, :].rearrange("p (q c) -> p q c", q=tiles), source(b, u, col)[:, j])\
                        .then_inc(sem(f"landed{slot}"), 16)

            first_units = filler(unit, ["lora"])
            first_units.drain()
            sp.dma_start(w2a2[0:64, :], dram["b_w2"].rearrange("l k n -> (l k) n")).then_inc(sem("w2_landed"), 16)
            sp.dma_start(w2a2[64:128, :], dram["b_a2"].rearrange("l k n -> (l k) n")).then_inc(sem("w2_landed"), 16)
            for name in phases:
                if name != "lora":
                    run(sp, unit, name, straight=("gate_a", "gate_2", "gate_3"))
            out_rows = out.rearrange("b (a p) d -> (b a) p d", p=P)
            for a in range(2):
                sp.wait_ge(sem("turn_copied"), TURNS["l"] + 4 * a + 4)
                sp.dma_start(out_rows[a], x_rows[:, a, :]).then_inc(sem("out_stored"), 16)
            sp.wait_ge(sem("out_stored"), 32)

        @block.gpsimd
        def _(pool):
            seen = Seen(pool)

            def link(ins):
                ins.then_inc(sem("pool_step"), 1)
                seen.need("pool_step")

            pool.memset(ident[:], 0.0)
            link(pool.memset(small[:], 0.0))
            link(pool.memset(small[:, 24:25], EPS))
            link(pool.memset(small[:, 25:26], GN_EPS))
            pool.affine_select(out=ident[:], in_=ident[:], compare_op=ALU.not_equal, fill=1.0, base=0,
                               pattern=[[-1, P]], channel_multiplier=1).then_inc(sem("ident_ready"), 1)
            pool.memset(ones[:], 1.0)
            link(pool.memset(blk[:], 0.0))
            link(pool.memset(blk[0:64, 0:64], 1.0))
            pool.memset(blk[64:128, 64:128], 1.0).then_inc(sem("ones_ready"), 1)
            pool.wait_ge(sem("ones_ready"), 1)
            for r in r_raw:
                pool.memset(r[:, :, 0:1], 0.0)
            pool.memset(lora[:, 0:1], 0.0)
            pool.memset(r_cs[:, :, 0:1], 0.0).then_inc(sem("zeros_ready"), 1)

            def mask(dst, *selects):
                work = m_work[:, 0:dst.shape[1]]
                link(pool.memset(work, 0.0))
                for k, (view, op, base, pattern, mult) in enumerate(selects):
                    v = view(work)
                    if op in (ALU.is_le, ALU.is_lt):
                        op = {ALU.is_le: ALU.is_ge, ALU.is_lt: ALU.is_gt}[op]
                        base, mult, pattern = -base, -mult, [[-step, count] for step, count in pattern]
                    link(pool.affine_select(out=v, in_=v, compare_op=op, fill=0.0 if k else 1.0, base=base,
                                            pattern=pattern, channel_multiplier=mult))
                link(pool.tensor_copy(dst[:], work))

            whole = lambda w: w
            mask(m_strict, (whole, ALU.is_le, 0, [[-1, P]], 1))
            mask(m_strict_t, (whole, ALU.is_le, 0, [[1, P]], -1))
            mask(m_incl_t, (whole, ALU.is_lt, 0, [[1, P]], -1))
            halves = lambda w: w.rearrange("p (b w) -> p b w", w=64)
            mask(m_gla, (whole, ALU.is_lt, 0, [[1, P]], -1), (halves, ALU.is_ge, 0, [[-64, 2], [0, 64]], 1))
            for l in range(LEVELS):
                w = 1 << l
                pairs = lambda v: v.rearrange("p (b w) -> p b w", w=w)
                pattern = [[-2 * w, P // (2 * w)], [0, w]]
                mask(m_level[l], (pairs, ALU.is_lt, -w, pattern, 1), (pairs, ALU.is_lt, -2 * w, pattern, 1))
                mask(m_level_t[l], (pairs, ALU.is_lt, 0, pattern, 1), (pairs, ALU.is_lt, -w, pattern, 1))
            pool.wait_ge(sem("norm_lo"), 4)
            pool.memset(r_g[:, :, :], 0.0)
            for z in (r_cm, r_ak, r_arb):
                pool.memset(z[:, :, :], 0.0)
            pool.memset(r_ark[:, :, :], 0.0).then_inc(sem("masks_ready"), 1)

            for p in range(KB):
                wait_evacuated(pool, phases[f"B{p}"][0])
                if p:
                    pool.wait_ge(sem("shift_read"), p)
                    pool.wait_ge(sem("y_lo"), p)
                raw = r_raw[p % 2]
                pool.tensor_tensor(r_d[:, :, :], raw[:, 0:3, 0:T], raw[:, 0:3, 1:T + 1], ALU.subtract)\
                    .then_inc(sem("shift_ready"), 1)
                for t in range(4):
                    pool.tensor_copy(r_x[:, t, :], ident[:])
                    ins = pool.tensor_copy(r_xt[:, t, :], ident[:])
                ins.then_inc(sem("inverse_reset"), 1)

            pool.wait_ge(sem("hn_done"), 4)
            pool.dma_start(ext[:, 0:256], dram["a_rel_bias"].rearrange("l h r -> (l h) r")[:, 1:257]).then_inc(sem("ext_landed"), 16)
            pool.wait_ge(sem("ext_landed"), 16)
            link(pool.tensor_scalar(ext[:, 256:384], ones[0:8, :], ext[:, 255:256], None, ALU.mult))
            pool.dma_start(rel.ap(), ext).then_inc(sem("rel_stored"), 16)
            pool.wait_ge(sem("rel_stored"), 16)
            h0 = HEAD0["a"]
            for h in range(8):
                if h >= 2:
                    pool.wait_ge(sem("scores_read"), h0 + h - 1)
                hank, bias = a_hankel[h % 2], a_bias[h % 2]
                src = bass.AP(rel, h * 384, [[1, P], [1, T]])
                pool.dma_start(hank, src).then_inc(sem(f"hankel_landed{h % 2}"), 16)
                pool.wait_ge(sem(f"hankel_landed{h % 2}"), 16 * (h // 2 + 1))
                pool.tensor_copy(bias[:, 0, 0:P], hank[:, 0:P][:, ::-1])
                pool.memset(bias[:, 0, P:T], MASKED)
                link(pool.tensor_copy(bias[:, 1, :], hank[:, ::-1]))
                link(pool.memset(bias[0:64, 0, 64:P], MASKED))
                pool.memset(bias[0:64, 1, 192:T], MASKED).then_inc(sem("bias_ready"), 1)
                pool.wait_ge(sem("bias_ready"), h + 1)
            pool.wait_ge(sem("y_lo"), HEAD0["a"] + 8 + KB)
            for a in range(2):
                pool.dma_start(mem_rows[a], dram["mem"].rearrange("b (a p) d -> (b a) p d", p=P)[a])\
                    .then_inc(sem(f"mem_landed{a}"), 16)
            pool.memset(c_bias[:, :, :], 0.0).then_inc(sem("c_bias_ready"), 1)
            pool.wait_ge(sem("norm_lo"), 8)
            pool.dma_start(l_up[0:16, :], dram["gla_w_up_2"].rearrange("l r n -> (l r) n")).then_inc(sem("up_landed"), 16)
            link(pool.iota(q_dist[:, :, :], pattern=[[-P, 2], [1, T]], base=0, channel_multiplier=-1,
                           allow_small_or_imprecise_dtypes=True))
            link(pool.affine_select(out=q_dist[:, :, :], in_=q_dist[:, :, :], compare_op=ALU.is_ge, fill=MASKED,
                                    base=0, pattern=[[P, 2], [-1, T]], channel_multiplier=1))
            h0 = HEAD0["q"]
            for h in range(8):
                if h >= 2:
                    pool.wait_ge(sem("scores_read"), h0 + h - 1)
                pool.tensor_scalar(q_bias[h % 2][:, :, :], q_dist[:, :, :], 2.0 ** -(h + 1), None, ALU.mult)\
                    .then_inc(sem("bias_ready"), 1)
            pool.wait_ge(sem("turn_copied"), TURNS["l"])
            pool.memset(l_at[:, :, :], 0.0)
            pool.memset(v_cu[:, 0:2], 0.0).then_inc(sem("gla_zeros"), 1)

        @block.scalar
        def _(act):
            seen = Seen(act)

            def root(dst, src, eps=EPS):
                at = {EPS: 24, GN_EPS: 25, 0.0: 26}[eps]
                act.activation(dst, src, ACT.Sqrt, bias=small[:, at:at + 1]).then_inc(sem("root_ready"), 1)

            def hi(n, i=None, per=0):
                slot = n % RING
                if n >= RING:
                    act.wait_ge(sem("unit_used"), on(i, n - RING + 1, per))
                act.wait_ge(sem(f"landed{slot}"), on(i, landed[n], 16 * per // RING))
                size = unit_size(n)
                act.activation(w_hi[:, slot, 0:size], w_raw[:, slot, 0:size], ACT.Copy).then_inc(sem("hi_done"), 1)

            def flat(v, at, i, each, size=UNIT):
                return v[:, at:at + size] if i is None else v[:, bass.ds(i * each + at, size)]

            def evacuate(m, i, per, body):
                b, g = blocks[m], gp[:, m % 2, :]
                done = sem(f"evacuated{m % 2}")
                kind, a = b.evac, b.arg
                if kind == "merge_c":
                    merged_high(a, 0, i, body)
                if kind in ("merge0", "merge", "merge_c", "residual"):
                    return
                act.wait_ge(sem("unit_used"), on(i, last_unit(m) + 1, per))
                tiles = g.rearrange("p (a b) -> p a b", b=T)
                if kind == "lora":
                    act.activation(lora[:, 1:T + 1], g[:, 0:T], ACT.Copy).then_inc(done, 1)
                elif kind == "rwkv":
                    if a >= 2:
                        act.wait_ge(sem("y_lo"), a - 1)
                    raw = r_raw[a % 2]
                    act.activation(raw[:, 0:3, 1:T + 1], tiles[:, 0:3, :], ACT.Copy)
                    act.activation(raw[:, 3, 1:T + 1], tiles[:, 3, :], ACT.Silu).then_inc(done, 1)
                elif kind == "a_cols":
                    dst = (a_q, a_k, a_vraw, a_z)[a // 2][:, 4 * (a % 2):4 * (a % 2) + 4, :]
                    act.activation(dst, tiles, ACT.Silu if a >= 6 else ACT.Copy).then_inc(done, 1)
                elif kind == "c_cols":
                    dst = (c_q, c_z)[a // 2][:, 4 * (a % 2):4 * (a % 2) + 4, :]
                    act.activation(dst, tiles, ACT.Silu if a >= 2 else ACT.Copy).then_inc(done, 1)
                elif kind == "l_cols":
                    dst = (l_q[:, :, :], l_k[:, :, :], l_vraw[:, 0:4, :], l_vraw[:, 4:8, :], l_z[:, 0:4, :], l_z[:, 4:8, :])[a]
                    act.activation(dst, tiles, ACT.Silu if a >= 4 else ACT.Copy).then_inc(done, 1)
                elif kind == "mem":
                    dst = (c_k, c_vraw)[a // 2][:, 4 * (a % 2):4 * (a % 2) + 4, :]
                    act.activation(dst, tiles, ACT.Copy).then_inc(done, 1)
                elif kind == "gla_down":
                    act.activation(l_down, g[:, 0:T], ACT.Copy).then_inc(done, 1)
                elif kind == "conv":
                    if a >= 2:
                        act.wait_ge(sem("conv_done"), a - 1)
                    act.activation(v_raw[a % 2][:, :, :], tiles[:, 0:3, :], ACT.Copy).then_inc(done, 1)
                elif kind == "gate":
                    wait_evacuated(act, m - 1, i, body)
                    act.activation(sig, g, ACT.Sigmoid).then_inc(done, 1)
                elif kind == "gate_c":
                    act.activation(flat(sig_c, a * UNIT, i, body * UNIT), g, ACT.Sigmoid).then_inc(done, 1)
                elif kind == "q_cols":
                    act.activation(flat(q_all, a * UNIT, i, body * UNIT), g, ACT.Copy).then_inc(done, 1)
                elif kind == "ffn_gate":
                    wait_evacuated(act, m - 1, i, body)
                    act.activation(f_t[:, 0, :], g, ACT.Silu).then_inc(done, 1)
                elif kind == "ffn_up":
                    act.wait_ge(sem("ffn_prod"), on(i, 1, 1))
                    dst = f_hi[:].rearrange("p a b -> p (a b)")
                    act.activation(flat(dst, 0, i, UNIT), f_t[:, 1, :], ACT.Copy).then_inc(sem("ffn_hi"), 1)

            def merged_high(q, before, i, each):
                act.wait_ge(sem("added"), on(i, 2 * before + 4 + q + 1, each))
                at = q * UNIT
                act.activation(flat(h_hi[:].rearrange("p a b -> p (a b)"), at, i, each * UNIT), flat(mg, at, i, each * UNIT), ACT.Copy)\
                    .then_inc(sem("merged_hi"), 1)

            def unit(n, i=None, per=0, body=0):
                if n + LEAD < n_units:
                    hi(n + LEAD, i, per)
                m, _ = units[n]
                if n == last_unit(m):
                    evacuate(m, i, per, body)

            def norm(ready, sq=n_sq):
                for q in range(4):
                    ready(q)
                    if q >= len(sq):
                        act.wait_ge(sem("norm_sq_used"), act_n["norm"] * 4 + q - len(sq) + 1)
                    act.activation(sq[q % len(sq)], x_t[:, 4 * q:4 * q + 4, :].rearrange("p a b -> p (a b)"), ACT.Square,
                                   scale=D ** -0.5).then_inc(sem("norm_sq"), 1)
                act_n["norm"] += 1
                act.wait_ge(sem("norm_sq_used"), 4 * act_n["norm"])
                root(area(76, T), psC[:, 0:T])

            def norm_beside(name, sq=None):
                fill = filler(unit, [name])

                def ready(q):
                    fill(blocks[phases[name][0]].kt // 2)
                    wait_evacuated(act, phases[name][0] + q)
                norm(ready, sq or n_sq)

            act_n = Counter()

            def split(h_dst, src, ready, done, quarters=4):
                for q in range(quarters):
                    seen.need(ready)
                    act.activation(h_dst(q), src(q), ACT.Copy).then_inc(sem(done), 1)

            def h_part(v):
                return lambda q: v[:, 4 * q:4 * q + 4, :].rearrange("p a b -> p (a b)")

            def heads_norm(src, size, buf, rs, fill, fills, ready=lambda half: None):
                for half in range(2):
                    ready(half)
                    if act_n["hn"]:
                        act.wait_ge(sem("hn_sq_used"), act_n["hn"])
                    act_n["hn"] += 1
                    act.activation(buf, src[:, 4 * half:4 * half + 4, :].rearrange("p a b -> p (a b)"), ACT.Square,
                                   scale=size ** -0.5).then_inc(sem("hn_sq"), 1)
                    act.wait_ge(sem("hn_sq_used"), act_n["hn"])
                    if act_n["hn"] > 1:
                        act.wait_ge(sem("hn_done"), act_n["hn"] - 1)
                    w = UNIT * 128 // size
                    root(rs[:, 0:w], psCD[:, 0:w])
                    fill(fills)

            def attention(which, n_heads, dt, fill, fills):
                h0 = HEAD0[which]
                for h in range(n_heads + 1):
                    if h < n_heads:
                        g = h0 + h
                        act.wait_ge(sem("max_ready"), g + 1)
                        s = att_s[g % 2]
                        for tt in range(2):
                            k = 2 * (g % 2) + tt
                            ins = act.activation(s[:, tt, :], s[:, tt, :], ACT.Exp, bias=small[:, k:k + 1],
                                                 accum_out=small[:, 4 + k:5 + k])
                        ins.then_inc(sem("exp_done"), 1)
                    if h:
                        split_y(g0=h - 1, dt=dt)
                    fill(fills)

            def split_y(g0, dt):
                seen.need("y_t")
                act.activation(y_hi[:, g0 * dt:g0 * dt + dt, :].rearrange("p a b -> p (a b)"), att_t[:, 0:dt * T],
                               ACT.Copy).then_inc(sem("y_hi"), 1)

            def pair(p, fill):
                act.wait_ge(sem("lora_z"), p + 1)
                act.activation(r_sg, psA[:, 0:T], ACT.Sigmoid, bias=g2("b_w0", p))
                act.activation(r_aa, psA[:, T:2 * T], ACT.Sigmoid, bias=g2("b_a0", p)).then_inc(sem("sigmoids"), 1)
                fill()
                act.wait_ge(sem("kk_ready"), p + 1)
                act.activation(r_sq, r_kk, ACT.Square).then_inc(sem("kk_sq"), 1)
                fill()
                act.wait_ge(sem("kk_sum"), p + 1)
                root(r_rs, psB[:, 0:T], 0.0)
                act.wait_ge(sem("mid_ready"), p + 1)
                for c in range(2):
                    act.activation(r_e1[:, c, :], r_cs[:, c, :], ACT.Exp, bias=small[:, 16 + c:17 + c], scale=-KAPPA)
                    ins = act.activation(r_e2[:, c, :], r_cs[:, c, :], ACT.Exp, bias=small[:, 18 + c:19 + c], scale=KAPPA)
                ins.then_inc(sem("decays"), 1)
                fill(3)
                for l in range(1, LEVELS):
                    act.wait_ge(sem("g_done"), p * (LEVELS - 1) + l)
                    act.activation(one_of_pair(r_g, l, 1), packed(psB, l), ACT.Copy).then_inc(sem("g_read"), 1)
                    fill()
                fill(2)
                act.wait_ge(sem("o_done"), p + 1)
                act.activation(r_o, psB[:, 0:T], ACT.Copy).then_inc(sem("o_read"), 1)
                fill()
                act.wait_ge(sem("dev_ready"), p + 1)
                act.activation(r_sq, r_dd, ACT.Square, scale=1.0 / 8).then_inc(sem("dev_sq"), 1)
                act.wait_ge(sem("var_done"), p + 1)
                root(r_aa, psC[:, T:2 * T], GN_EPS)
                fill()
                act.wait_ge(sem("rwkv_t"), p + 1)
                act.activation(y_hi[:, p, :], r_t, ACT.Copy).then_inc(sem("y_hi"), 1)

            for n in range(LEAD):
                hi(n)
            norm(lambda q: act.wait_ge(sem("turn_copied"), 2 * q + 2))
            split(h_part(h_hi), lambda q: n_sq[q % 2], "norm_t", "norm_hi")
            fill = filler(unit, ["lora", "B0"])
            fill(7)
            act.wait_ge(sem("lora_shifted"), 1)
            act.activation(lora_x[0:64, :], lora_x[0:64, :], ACT.Tanh).then_inc(sem("lora_ready"), 1)
            fill.drain()
            for p in range(KB):
                fill = filler(unit, [f"B{p + 1}", f"A{p}"] if p + 1 < KB else [f"A{p}", "gate_b0"])
                pair(p, fill)
                fill.drain()
            fill = filler(unit, ["gate_b"])
            for src in (a_q, a_k):
                heads_norm(src, 128, hn_sq, hn_rs, fill, 5)
            fill.drain()
            fill = filler(unit, ["C"])
            attention("a", 8, 1, fill, 4)
            fill.drain()
            fill = filler(unit, ["gate_a"])
            fill(8)
            for a in range(2):
                act.wait_ge(sem(f"mem_landed{a}"), 16)
                for q in range(2):
                    if a:
                        act.wait_ge(sem("mem_sums"), q + 1)
                    act.activation(mem_t[q], mem_rows[a][:, q * UNIT:(q + 1) * UNIT], ACT.Square, scale=D ** -0.5,
                                   accum_out=small[:, 20 + 2 * a + q:21 + 2 * a + q]).then_inc(sem("mem_sums"), 1)
                fill(1)
            act.wait_ge(sem("mem_mean"), 1)
            root(small[:, 28:30], small[:, 28:30])
            fill.drain()
            act.wait_ge(sem("unit_used"), first[phases["mem"][0]])
            for q in range(4):
                act.wait_ge(sem("turn_copied"), TURNS["a"] + 2 * q + 2)
                act.activation(h_part((y_hi, y_lo)[q // 2])(q % 2), mem_t[q % 2], ACT.Copy).then_inc(sem("mem_hi"), 1)
            run(act, unit, "mem")
            wait_evacuated(act, phases["mem"][0])
            fill = filler(unit, ["gate_c"])
            heads_norm(c_q, 256, c_sq, c_rs, fill, 2)
            heads_norm(c_k, 256, c_sq, c_rs, fill, 2, lambda half: wait_evacuated(act, phases["mem"][0] + half))
            fill(2)
            attention("c", 4, 2, fill, 6)
            fill.drain()
            run(act, unit, "up_c")
            norm_beside("o")
            split(h_part(h_hi), lambda q: n_sq[q % 2], "norm_t", "norm_hi")
            run(act, unit, "Q")
            fill = filler(unit, ["L", "down"])
            attention("q", 8, 1, fill, 6)
            fill.drain()
            run(act, unit, "gate_1")
            fill = filler(unit, [f"V{p}" for p in range(KB)])
            act.wait_ge(sem("gla_min"), 1)
            for h in range(4):
                ins = act.activation(l_exp[:, h * T:(h + 1) * T], ps[:, h // 2, h % 2 * T:(h % 2 + 1) * T], ACT.Abs, bias=g2("gla_b_2", h))
            ins.then_inc(sem("act_step"), 1)
            seen.need("act_step")
            act.activation(l_exp, l_exp, ACT.Exp, scale=-1.0).then_inc(sem("act_step"), 1)
            seen.need("act_step")
            act.activation(l_exp, l_exp, ACT.Ln, bias=1.0).then_inc(sem("gla_ln"), 1)
            fill(4)

            def decays(h):
                cs = l_cs[:, h * T:(h + 1) * T]
                act.activation(l_e1, cs, ACT.Exp, scale=1.0 / 16)
                act.activation(l_e2, cs, ACT.Exp, scale=-1.0 / 16).then_inc(sem("gla_decays"), 1)

            act.wait_ge(sem("gla_cs"), 1)
            decays(0)
            for h in range(4):
                fill(5)
                act.wait_ge(sem("gla_o"), h + 1)
                act.activation(l_sq[:, :, :].rearrange("p a b -> p (a b)"), psC, ACT.Square, scale=1.0 / 16).then_inc(sem("gla_sq"), 1)
                fill(5)
                act.wait_ge(sem("gla_ss"), h + 1)
                root(l_rs, psD[:, 0:T])
                fill(2)
                seen.need("gla_y")
                act.activation(y_hi[:, 2 * h:2 * h + 2, :].rearrange("p a b -> p (a b)"), l_y, ACT.Copy).then_inc(sem("y_hi"), 1)
                if h < 3:
                    decays(h + 1)
                fill(3)
            fill.drain()
            run(act, unit, "gate_2")
            act.wait_ge(sem("unit_used"), last_unit(phases["gate_3"][0] - 1) + 1)
            for q in range(2):
                act.wait_ge(sem("conv_done"), 4 * q + 4)
                act.activation(y_hi[:, 4 * q:4 * q + 4, :].rearrange("p a b -> p (a b)"),
                               v_y[:, 4 * q:4 * q + 4, :].rearrange("p a b -> p (a b)"), ACT.Copy).then_inc(sem("y_hi"), 1)
            run(act, unit, "gate_3")
            for q in range(4):
                merged_high(q, 4, None, 0)
            norm_beside("o2")
            split(h_part(h_hi), lambda q: n_sq[q % 2], "norm_t", "norm_hi")
            run(act, unit, "ffn")
            norm_beside("ffn_down", last_sq)

        @block.vector
        def _(dve):
            seen = Seen(dve)

            def link(ins):
                ins.then_inc(sem("dve_step"), 1)
                seen.need("dve_step")

            def inverse_root(dst, least=None):
                seen.need("root_ready")
                if least is not None:
                    link(dve.tensor_scalar(dst, dst, least, None, ALU.max))
                link(dve.reciprocal(dst, dst))

            def lo(n, i=None, per=0):
                slot = n % RING
                dve.wait_ge(sem("hi_done"), on(i, n + 1, per))
                size = unit_size(n)
                dve.tensor_tensor(w_lo[:, slot, 0:size], w_raw[:, slot, 0:size], w_hi[:, slot, 0:size].bitcast(F32), ALU.subtract)\
                    .then_inc(sem("lo_done"), 1)

            def flat(v, at, i, each, size=UNIT):
                return v[:, at:at + size] if i is None else v[:, bass.ds(i * each + at, size)]

            def evacuate(m, i, per, body):
                b, g = blocks[m], gp[:, m % 2, :]
                done = sem(f"evacuated{m % 2}")
                kind, a = b.evac, b.arg
                if kind in ("merge0", "merge", "merge_c", "residual", "ffn_up"):
                    dve.wait_ge(sem("unit_used"), on(i, last_unit(m) + 1, per))
                if kind in ("merge0", "merge"):
                    wait_evacuated(dve, m - 1, i, body)
                    each = body // 2 * UNIT
                    if kind == "merge0":
                        dve.tensor_tensor(flat(mg, a // 2 * UNIT, i, each), sig, g, ALU.mult).then_inc(done, 1)
                        return
                    dve.tensor_tensor(prod, sig, g, ALU.mult).then_inc(done, 1)
                    wait_evacuated(dve, m, i, body)
                    part = flat(mg, a // 2 * UNIT, i, each)
                    dve.tensor_tensor(part, part, prod, ALU.add).then_inc(sem("added"), 1)
                elif kind == "merge_c":
                    each = body * UNIT
                    dve.tensor_tensor(prod, flat(sig_c, a * UNIT, i, each), g, ALU.mult).then_inc(done, 1)
                    wait_evacuated(dve, m, i, body)
                    part = flat(mg, a * UNIT, i, each)
                    dve.tensor_tensor(part, part, prod, ALU.add).then_inc(sem("added"), 1)
                    merged_low(a, 0, i, body)
                elif kind == "residual":
                    part = flat(x_t[:].rearrange("p a b -> p (a b)"), a * UNIT, i, body * UNIT)
                    dve.tensor_tensor(part, part, g, ALU.add).then_inc(done, 1)
                elif kind == "ffn_up":
                    wait_evacuated(dve, m - 1, i, body)
                    dve.tensor_tensor(f_t[:, 1, :], f_t[:, 0, :], g, ALU.mult).then_inc(sem("ffn_prod"), 1)
                    dve.wait_ge(sem("ffn_hi"), on(i, 1, 1))
                    hi_part = flat(f_hi[:].rearrange("p a b -> p (a b)"), 0, i, UNIT)
                    lo_part = flat(f_lo[:].rearrange("p a b -> p (a b)"), 0, i, UNIT)
                    dve.tensor_tensor(lo_part, f_t[:, 1, :], hi_part.bitcast(F32), ALU.subtract).then_inc(done, 1)
                elif kind == "conv":
                    wait_evacuated(dve, m)
                    if a == 0:
                        dve.wait_ge(sem("gla_zeros"), 1)
                    raw = v_raw[a % 2]
                    link(dve.tensor_tensor(v_cu[:, 2:T + 2], raw[:, 1, :], raw[:, 2, :], ALU.mult))
                    link(dve.tensor_scalar(v_t, v_cu[:, 0:T], g2("conv_w_2", a), None, ALU.mult))
                    link(dve.scalar_tensor_tensor(v_t, v_cu[:, 1:T + 1], g2("conv_w_2", 8 + a), v_t, ALU.mult, ALU.add))
                    link(dve.scalar_tensor_tensor(v_t, v_cu[:, 2:T + 2], g2("conv_w_2", 16 + a), v_t, ALU.mult, ALU.add))
                    dve.tensor_tensor(v_y[:, a, :], v_t, raw[:, 0, :], ALU.mult).then_inc(sem("conv_done"), 1)

            def merged_low(q, before, i, each):
                dve.wait_ge(sem("merged_hi"), on(i, before + q + 1, each))
                at = q * UNIT
                hi_part = flat(h_hi[:].rearrange("p a b -> p (a b)"), at, i, each * UNIT)
                lo_part = flat(h_lo[:].rearrange("p a b -> p (a b)"), at, i, each * UNIT)
                dve.tensor_tensor(lo_part, flat(mg, at, i, each * UNIT), hi_part.bitcast(F32), ALU.subtract).then_inc(sem("merged_lo"), 1)

            def unit(n, i=None, per=0, body=0):
                if n + LEAD < n_units:
                    lo(n + LEAD, i, per)
                m, _ = units[n]
                if n == last_unit(m):
                    if blocks[m].evac in ("merge", "merge_c"):
                        dve.wait_ge(sem("lo_done"), on(i, n + LEAD + 1, per))
                    evacuate(m, i, per, body)

            dve_n = Counter()

            def turn(dsts):
                for dst in dsts:
                    seen.need("turned")
                    dve.tensor_copy(dst, ps[:, (seen.n["turned"] - 1) % 2, :]).then_inc(sem("turn_copied"), 1)

            def norm(gain, last=False):
                rs = area(76, T)
                inverse_root(rs)

                def scaled(q):
                    for t in range(4):
                        src = x_t[:, 4 * q + t, :]
                        dst = src if last else n_sq[q % 2][:, t * T:(t + 1) * T]
                        ins = dve.scalar_tensor_tensor(dst, src, g1(gain, 4 * q + t), rs, ALU.mult, ALU.mult)
                    ins.then_inc(sem("norm_t"), 1)

                def low(q):
                    seen.need("norm_hi")
                    h = h_hi[:, 4 * q:4 * q + 4, :].rearrange("p a b -> p (a b)")
                    l = h_lo[:, 4 * q:4 * q + 4, :].rearrange("p a b -> p (a b)")
                    dve.tensor_tensor(l, n_sq[q % 2], h.bitcast(F32), ALU.subtract).then_inc(sem("norm_lo"), 1)

                for q in range(4):
                    if q >= 2 and not last:
                        dve.wait_ge(sem("norm_lo"), dve_n["norm_lo"] + q - 1)
                    scaled(q)
                    if q and not last:
                        low(q - 1)
                if not last:
                    low(3)
                dve_n["norm_lo"] += 4

            def heads_norm(dst, gain, per_head, rs, fill, fills):
                for half in range(2):
                    seen.need("root_ready")
                    for hd in range(4 // per_head):
                        r = rs[:, hd * T:(hd + 1) * T]
                        link(dve.reciprocal(r, r))
                        for t in range(hd * per_head, (hd + 1) * per_head):
                            v = dst[:, 4 * half + t, :]
                            ins = dve.scalar_tensor_tensor(v, v, g2(gain, t % per_head), r, ALU.mult, ALU.mult)
                        if hd == 4 // per_head - 1:
                            ins.then_inc(sem("hn_done"), 1)
                        fill(1)
                    fill(fills - 4 // per_head)

            def attention(which, n_heads, dt, biases, z, fill, fills):
                h0 = HEAD0[which]
                scale = (dt * P) ** -0.5

                def scores(h):
                    g = h0 + h
                    s, k = att_s[g % 2], 2 * (g % 2)
                    dve.wait_ge(sem("scores_done"), g + 1)
                    if which == "c":
                        dve.wait_ge(sem("c_bias_ready"), 1)
                    else:
                        dve.wait_ge(sem("bias_ready"), g + 1 - (4 if which == "q" else 0))
                    dve.scalar_tensor_tensor(s[:, :, :].rearrange("p a b -> p (a b)"), ps[:, 2 + g % 2, :], scale,
                                             biases[h % len(biases)][:, :, :].rearrange("p a b -> p (a b)"),
                                             ALU.mult, ALU.add).then_inc(sem("scores_read"), 1)
                    dve.wait_ge(sem("scores_read"), g + 1)
                    link(dve.tensor_reduce(small[:, 8 + k:10 + k], s[:, :, :], AX, ALU.max))
                    dve.tensor_scalar(small[:, k:k + 2], small[:, 8 + k:10 + k], -1.0, None, ALU.mult).then_inc(sem("max_ready"), 1)

                scores(0)
                for h in range(n_heads):
                    g = h0 + h
                    s, k = att_s[g % 2], 2 * (g % 2)
                    if h + 1 < n_heads:
                        scores(h + 1)
                    dve.wait_ge(sem("exp_done"), g + 1)
                    link(dve.reciprocal(small[:, 4 + k:6 + k], small[:, 4 + k:6 + k]))
                    for tt in range(2):
                        ins = dve.tensor_scalar(s[:, tt, :], s[:, tt, :], small[:, 4 + k + tt:5 + k + tt], None, ALU.mult)
                    ins.then_inc(sem("p_ready"), 1)
                    fill(fills // 2)
                    dve.wait_ge(sem("p_turned"), g + 1)
                    if g:
                        dve.wait_ge(sem("pv_done"), g)
                    dve.tensor_copy(att_pt[:, :, :].rearrange("p a b -> p (a b)"), psA).then_inc(sem("pt_copied"), 1)
                    fill(fills - fills // 2)
                    dve.wait_ge(sem("pv_done"), g + 1)
                    zz = z[:, h * dt:h * dt + dt, :].rearrange("p a b -> p (a b)") if z is not None else None
                    if z is None:
                        dve.tensor_copy(att_t[:, 0:dt * T], psB[:, 0:dt * T]).then_inc(sem("y_t"), 1)
                    else:
                        dve.tensor_tensor(att_t[:, 0:dt * T], psB[:, 0:dt * T], zz, ALU.mult).then_inc(sem("y_t"), 1)
                    low_y(y_hi[:, h * dt:h * dt + dt, :], y_lo[:, h * dt:h * dt + dt, :], att_t[:, 0:dt * T])

            def low_y(h, l, src):
                seen.need("y_hi")
                if len(h.shape) == 3:
                    h, l = h.rearrange("p a b -> p (a b)"), l.rearrange("p a b -> p (a b)")
                dve.tensor_tensor(l, src, h.bitcast(F32), ALU.subtract).then_inc(sem("y_lo"), 1)

            def pair(p, fill):
                raw = r_raw[p % 2]
                fl = lambda v: v[:, :, :].rearrange("p a b -> p (a b)")
                two = lambda v: v.rearrange("p (a b) -> p a b", b=CHUNK)
                dve.wait_ge(sem("shift_ready"), p + 1)
                wait_evacuated(dve, phases[f"B{p}"][0])
                for q in (1, 0, 2):
                    ins = dve.scalar_tensor_tensor(r_rkv[:, q, :], r_d[:, q, :], g2("b_mu_rkv", 8 * q + p),
                                                   raw[:, q, 1:T + 1], ALU.mult, ALU.add)
                ins.then_inc(sem("shift_read"), 1)
                dve.wait_ge(sem("shift_read"), p + 1)
                r, k, v = (r_rkv[:, q, :] for q in range(3))
                dve.tensor_scalar(r_kk, k, g2("b_k_k", p), None, ALU.mult).then_inc(sem("kk_ready"), 1)
                fill()
                dve.wait_ge(sem("sigmoids"), p + 1)
                for c in range(2):
                    ins = dve.tensor_tensor_scan(r_cs[:, c, 1:CHUNK + 1], ones[:], r_sg[:, c * CHUNK:(c + 1) * CHUNK],
                                                 0.0, ALU.mult, ALU.add)
                link(ins)
                mid = r_cs[:, :, CHUNK // 2]
                dve.tensor_scalar(small[:, 16:18], mid, KAPPA, None, ALU.mult)
                dve.tensor_scalar(small[:, 18:20], mid, -KAPPA, None, ALU.mult).then_inc(sem("mid_ready"), 1)
                fill()
                link(dve.tensor_scalar(r_af, r_aa, g2("b_k_a", p), one_minus_ka[:, p:p + 1], ALU.mult, ALU.add))
                link(dve.tensor_tensor(r_o2, k, r_af, ALU.mult))
                link(dve.scalar_tensor_tensor(r_rk, r, g2("b_r_k", p), r_o2, ALU.mult, ALU.mult))
                inverse_root(r_rs, 1e-12)
                link(dve.tensor_tensor(r_kk, r_kk, r_rs, ALU.mult))
                link(dve.tensor_tensor(r_aa, r_kk, r_aa, ALU.mult))
                dve.wait_ge(sem("decays"), p + 1)
                dve.scalar_tensor_tensor(two(r_at), two(r_kk), -1.0, r_e1[:, :, 0:CHUNK], ALU.mult, ALU.mult)
                dve.tensor_tensor(two(r_bt), two(r_aa), r_e2[:, :, 1:CHUNK + 1], ALU.mult).then_inc(sem("ab_ready"), 1)
                dve.tensor_tensor(two(r_kt), two(r_o2), r_e2[:, :, 1:CHUNK + 1], ALU.mult)
                dve.tensor_tensor(two(r_rt), two(r), r_e1[:, :, 1:CHUNK + 1], ALU.mult).then_inc(sem("kr_ready"), 1)
                fill(3)
                if p == 0:
                    dve.wait_ge(sem("masks_ready"), 1)
                dve.wait_ge(sem("inverse_reset"), p + 1)
                dve.wait_ge(sem("prod_abt"), p + 1)
                bank = lambda v: v.rearrange("p (a b) -> p a b", b=P)
                dve.copy_predicated(one_of_pair(r_xt, 0, 1), level_mask(m_level_t[0], 0), one_of_pair(bank(psA), 0, 1)).then_inc(sem("abt_read"), 1)
                dve.wait_ge(sem("prod_ab"), p + 1)
                dve.copy_predicated(one_of_pair(r_x, 0, 0), level_mask(m_level[0], 0), one_of_pair(bank(psD), 0, 0))
                dve.copy_predicated(r_cm[:, :, :], mask4(m_strict), bank(psD)).then_inc(sem("ab_read"), 1)
                dve.wait_ge(sem("prod_ak"), p + 1)
                dve.copy_predicated(r_ak[:, :, :], mask4(m_strict_t), bank(psC)).then_inc(sem("ak_read"), 1)
                dve.wait_ge(sem("prod_rb"), p + 1)
                dve.copy_predicated(r_arb[:, :, :], mask4(m_incl_t), bank(psA)).then_inc(sem("rb_read"), 1)
                for l in range(1, LEVELS):
                    n = p * (LEVELS - 1) + l
                    fill()
                    dve.wait_ge(sem("xg_done"), n)
                    ins = dve.copy_predicated(one_of_pair(r_xt, l, 1), level_mask(m_level_t[l], l), packed(psC, l))
                    if l < LEVELS - 1:
                        ins = dve.copy_predicated(one_of_pair(r_x, l, 0), level_mask(m_level[l], l), packed(psD, l))
                    ins.then_inc(sem("x_ready"), 1)
                    if l == 1:
                        dve.wait_ge(sem("prod_rk"), p + 1)
                        dve.copy_predicated(r_ark[:, :, :], mask4(m_incl_t), bank(psA)).then_inc(sem("rk_read"), 1)
                    if l == 2:
                        dve.wait_ge(sem("vbk_turned"), p + 1)
                        dve.tensor_copy(fl(r_vbk), psA).then_inc(sem("vbk_ready"), 1)
                for c in range(2):
                    dve.wait_ge(sem("w_done"), 2 * p + c + 1)
                    dve.tensor_copy(r_w[:, 0:P], psA[:, 0:P]).then_inc(sem("w_read"), 1)
                    if c == 0:
                        fill()
                    dve.wait_ge(sem("u_done"), 2 * p + c + 1)
                    dve.tensor_copy(r_u[:, c * P:(c + 1) * P], psA[:, P:2 * P]).then_inc(sem("u_read"), 1)
                    if c == 0:
                        dve.wait_ge(sem("s_done"), p + 1)
                        dve.tensor_scalar(r_s, psD[:, 0:64], r_e1[:, 0, CHUNK:CHUNK + 1], r_e2[:, 1, 0:1], ALU.mult, ALU.mult)\
                            .then_inc(sem("s_read"), 1)
                fill()
                dve.wait_ge(sem("mean_done"), p + 1)
                dve.scalar_tensor_tensor(r_dd, psC[:, 0:T], -1.0 / 64, r_o, ALU.mult, ALU.add).then_inc(sem("dev_ready"), 1)
                dve.wait_ge(sem("bonus_done"), p + 1)
                dve.wait_ge(sem("dev_ready"), p + 1)
                dve.tensor_tensor(r_kk, psD[:, 0:T], v, ALU.mult)
                fill()
                inverse_root(r_aa)
                link(dve.tensor_tensor(r_dd, r_dd, r_aa, ALU.mult))
                link(dve.tensor_scalar(r_dd, r_dd, g2("b_ln_w", p), g2("b_ln_b", p), ALU.mult, ALU.add))
                link(dve.tensor_tensor(r_dd, r_dd, r_kk, ALU.add))
                dve.tensor_tensor(r_t, r_dd, raw[:, 3, 1:T + 1], ALU.mult).then_inc(sem("rwkv_t"), 1)
                fill()
                low_y(y_hi[:, p, :], y_lo[:, p, :], r_t)

            for n in range(LEAD):
                lo(n)
            turn([x_t[:, 2 * g:2 * g + 2, :].rearrange("p a b -> p (a b)") for g in range(8)])
            dve.wait_ge(sem("vec_turned"), 1)
            dve.tensor_copy(vec1[:, 0:n_rows1], psC[:, 0:n_rows1])
            link(dve.tensor_copy(vec2[:, 0:n_rows2], psC[:, P:P + n_rows2]))
            dve.tensor_scalar(one_minus_ka[:], vec2[:, v2["b_k_a"]:v2["b_k_a"] + 8], -1.0, 1.0, ALU.mult, ALU.add)\
                .then_inc(sem("vec_ready"), 1)
            dve.wait_ge(sem("vec_ready"), 1)
            norm("norm_g")
            fill = filler(unit, ["lora", "B0"])
            fill(4)
            wait_evacuated(dve, 0)
            dve.wait_ge(sem("zeros_ready"), 1)
            link(dve.tensor_tensor(lora_x, lora[:, 0:T], lora[:, 1:T + 1], ALU.subtract))
            dve.scalar_tensor_tensor(lora_x, lora_x, g2("b_mu_w"), lora[:, 1:T + 1], ALU.mult, ALU.add).then_inc(sem("lora_shifted"), 1)
            fill.drain()
            for p in range(KB):
                fill = filler(unit, [f"B{p + 1}", f"A{p}"] if p + 1 < KB else [f"A{p}", "gate_b0"])
                pair(p, fill)
                fill.drain()
            values = lambda v: [v[:, tt, 512 * g:512 * g + 512] for tt in range(2) for g in range(2)]
            fill = filler(unit, ["gate_b"])
            heads_norm(a_q, "a_q_g", 1, hn_rs, fill, 5)
            heads_norm(a_k, "a_k_g", 1, hn_rs, fill, 5)
            turn(values(att_v))
            fill.drain()
            fill = filler(unit, ["C"])
            wait_evacuated(dve, phases["C"][0] - 1)
            attention("a", 8, 1, a_bias, a_z, fill, 4)
            fill.drain()
            fill = filler(unit, ["gate_a"])
            fill(10)
            dve.wait_ge(sem("mem_sums"), 4)
            sums = small[:, 20:24].rearrange("p (a b) -> p a b", b=2)
            dve.tensor_tensor(small[:, 28:30], sums[:, :, 0], sums[:, :, 1], ALU.add).then_inc(sem("mem_mean"), 1)
            inverse_root(small[:, 28:30])
            for a in range(2):
                dve.tensor_scalar(mem_rows[a], mem_rows[a], small[:, 28 + a:29 + a], None, ALU.mult).then_inc(sem("mem_scaled"), 1)
                fill(1)
            fill.drain()

            def mem_low(q):
                seen.need("mem_hi")
                h = (y_hi, y_lo)[q // 2][:, 4 * (q % 2):4 * (q % 2) + 4, :].rearrange("p a b -> p (a b)")
                l = mem_lo[:, 4 * q:4 * q + 4, :].rearrange("p a b -> p (a b)")
                dve.tensor_tensor(l, mem_t[q % 2], h.bitcast(F32), ALU.subtract).then_inc(sem("mem_lo"), 1)

            for q in range(4):
                if q >= 2:
                    dve.wait_ge(sem("mem_lo"), q - 1)
                for g in range(2):
                    seen.need("turned")
                    src = ps[:, (seen.n["turned"] - 1) % 2, :]
                    for t in range(2):
                        dst = mem_t[q % 2][:, g * 512 + t * T:g * 512 + (t + 1) * T]
                        ins = dve.tensor_scalar(dst, src[:, t * T:(t + 1) * T], g1("mem_norm_g", 4 * q + 2 * g + t), None, ALU.mult)
                    ins.then_inc(sem("turn_copied"), 1)
                if q:
                    mem_low(q - 1)
            mem_low(3)
            run(dve, unit, "mem")
            fill = filler(unit, ["gate_c"])
            heads_norm(c_q, "c_q_g", 2, c_rs, fill, 2)
            heads_norm(c_k, "c_k_g", 2, c_rs, fill, 2)
            turn(values(c_v))
            fill(2)
            attention("c", 4, 2, [c_bias], c_z, fill, 6)
            fill.drain()
            run(dve, unit, "up_c")

            run(dve, unit, "o")
            norm("norm1_w_2")
            run(dve, unit, "Q")
            turn(values(att_v))
            fill = filler(unit, ["L", "down"])
            attention("q", 8, 1, q_bias, None, fill, 6)
            fill.drain()
            run(dve, unit, "gate_1")
            turn(values(l_v))
            fill = filler(unit, [f"V{p}" for p in range(KB)])
            dve.wait_ge(sem("gla_z"), 1)
            for h in range(4):
                ins = dve.tensor_scalar(l_log[:, h * T:(h + 1) * T], ps[:, h // 2, h % 2 * T:(h % 2 + 1) * T], g2("gla_b_2", h), 0.0, ALU.add, ALU.min)
            ins.then_inc(sem("gla_min"), 1)
            dve.wait_ge(sem("gla_min"), 1)
            dve.wait_ge(sem("gla_ln"), 1)
            link(dve.tensor_tensor(l_log, l_log, l_exp, ALU.subtract))
            for c in range(16):
                ins = dve.tensor_tensor_scan(l_cs[:, 64 * c:64 * c + 64], ones[:, 0:64], l_log[:, 64 * c:64 * c + 64],
                                             0.0, ALU.mult, ALU.add)
            ins.then_inc(sem("gla_cs"), 1)
            fill(4)
            for h in range(4):
                dve.wait_ge(sem("gla_decays"), h + 1)
                dve.scalar_tensor_tensor(l_qin, l_q[:, h, :], P ** -0.5, l_e1, ALU.mult, ALU.mult)
                dve.tensor_tensor(l_kin, l_k[:, h, :], l_e2, ALU.mult).then_inc(sem("gla_in"), 1)
                fill(1)
                dve.wait_ge(sem("gla_a"), h + 1)
                if h == 0:
                    dve.wait_ge(sem("gla_zeros"), 1)
                dve.copy_predicated(l_at[:, :, :], mask4(m_gla, 2), psB[:, 0:T].rearrange("p (a b) -> p a b", b=P))
                dve.tensor_copy(l_kt[:, :, :].rearrange("p a b -> p (a b)"), psB[:, T:2 * T]).then_inc(sem("gla_a_read"), 1)
                for c in range(3):
                    dve.wait_ge(sem("gla_kv"), 3 * h + c + 1)
                    src = psA[:, T:2 * T] if c % 2 == 0 else psD[:, T:2 * T]
                    if c:
                        link(dve.tensor_tensor(l_kv, l_s[c - 1], src, ALU.add))
                        src = l_kv
                    dve.tensor_scalar(l_s[c], src, l_e1[:, 64 * c + 63:64 * c + 64], None, ALU.mult).then_inc(sem("gla_s"), 1)
                    if c < 2:
                        dve.wait_ge(sem("gla_s"), 3 * h + c + 1)
                fill(9)
                inverse_root(l_rs)
                for e in range(2):
                    ins = dve.scalar_tensor_tensor(l_y[:, e * T:(e + 1) * T], psC[:, e * T:(e + 1) * T],
                                                   g2("gla_norm_w_2", e), l_rs, ALU.mult, ALU.mult)
                link(ins)
                dve.tensor_tensor(l_y, l_y, l_z[:, 2 * h:2 * h + 2, :].rearrange("p a b -> p (a b)"), ALU.mult).then_inc(sem("gla_y"), 1)
                fill(2)
                low_y(y_hi[:, 2 * h:2 * h + 2, :], y_lo[:, 2 * h:2 * h + 2, :], l_y)
                fill(3)
            fill.drain()
            run(dve, unit, "gate_2")
            for q in range(2):
                low_y(y_hi[:, 4 * q:4 * q + 4, :], y_lo[:, 4 * q:4 * q + 4, :], v_y[:, 4 * q:4 * q + 4, :].rearrange("p a b -> p (a b)"))
            run(dve, unit, "gate_3")
            for q in range(4):
                merged_low(q, 4, None, 0)
            run(dve, unit, "o2")
            norm("norm2_w_2")
            run(dve, unit, "ffn")
            run(dve, unit, "ffn_down")
            norm("final_norm_w_2", last=True)
            for a in range(2):
                for g in range(4):
                    seen.need("turned")
                    ins = dve.tensor_copy(x_rows[:, a, 512 * g:512 * g + 512], ps[:, (seen.n["turned"] - 1) % 2, :])
                    ins.then_inc(sem("turn_copied"), 1)

        @block.tensor
        def _(pe):
            seen = Seen(pe)
            tiles_of = lambda v, n: [v[:, k, :] for k in range(n)]
            operands = {"h": (tiles_of(h_hi, KD), tiles_of(h_lo, KD)), "y": (tiles_of(y_hi, KB), tiles_of(y_lo, KB)),
                        "f": (tiles_of(f_hi, KF), tiles_of(f_lo, KF)),
                        "mem": (tiles_of(y_hi, KB) + tiles_of(y_lo, KB), tiles_of(mem_lo, KD))}

            def unit(n, i=None, per=0, body=0, part=None):
                m, u = units[n]
                b, slot, s = blocks[m], n % RING, m % 2
                k_tiles, tiles = KINDS[b.kind]
                x_hi, x_lo = operands[b.operand]
                if part != 1:
                    if u == 0 and m >= 2:
                        wait_evacuated(pe, m - 2, i, body)
                    pe.wait_ge(sem("lo_done"), on(i, n + 1, per))
                    if m == phases["ffn_down"][0] and (u + 1) * k_tiles > KF - 4:
                        wait_evacuated(pe, m - 1)
                    if m in operand_ready:
                        name, before, size = operand_ready[m]
                        pe.wait_ge(sem(name), before + (u * k_tiles + k_tiles - 1) // size + 1)
                last_k = b.kt - 1
                half = k_tiles // 2
                for j in {None: range(k_tiles), 0: range(half), 1: range(half, k_tiles)}[part]:
                    k = u * k_tiles + j
                    for c in range(tiles):
                        o = gp[:, s, c * T:(c + 1) * T]
                        at = (j * tiles + c) * P
                        wh, wl = w_hi[:, slot, at:at + P], w_lo[:, slot, at:at + P]
                        pe.matmul(o, wh, x_hi[k], start=(k == 0 and c % 2 == 0), stop=False, skip_group_check=True)
                        pe.matmul(o, wh, x_lo[k], start=False, stop=False, skip_group_check=True)
                        ins = pe.matmul(o, wl, x_hi[k], start=False, stop=(k == last_k), skip_group_check=True)
                if part != 0:
                    ins.then_inc(sem("unit_used"), 1)

            def fill_halves(names):
                todo = [(n, part) for name in names for n in range(first[phases[name][0]], last_unit(phases[name][0] + phases[name][1] * phases[name][2] - 1) + 1)
                        for part in range(2)]

                def fill(k=1):
                    for _ in range(int(2 * k)):
                        if todo:
                            n, part = todo.pop(0)
                            unit(n, part=part)
                fill.drain = lambda: fill(len(todo))
                return fill

            operand_ready = {
                phases["lora"][0]: ("norm_lo", 0, 4),
                phases["gate_b"][0]: ("y_lo", 0, 1),
                phases["gate_a"][0] + 1: ("y_lo", KB, 1),
                phases["mem"][0]: ("mem_lo", 0, 4),
                phases["up_c"][0]: ("y_lo", KB + 8, 2),
                phases["o"][0]: ("merged_lo", 0, 4),
                phases["Q"][0]: ("norm_lo", 4, 4),
                phases["o2"][0]: ("merged_lo", 4, 4),
                phases["ffn"][0]: ("norm_lo", 8, 4),
                phases["gate_3"][0] + 1: ("y_lo", KB + 24, 4)}

            def turn(batches):
                for tiles in batches:
                    if pe_n["turn"] >= 2:
                        pe.wait_ge(sem("turn_copied"), pe_n["turn"] - 1)
                    bank = ps[:, pe_n["turn"] % 2, :]
                    for j, src in enumerate(tiles):
                        ins = pe.transpose(bank[:, j * P:(j + 1) * P], src, ident[:])
                    ins.then_inc(sem("turned"), 1)
                    pe_n["turn"] += 1

            pe_n = Counter()

            def norm(fill=None, block_units=8, sq=n_sq):
                for q in range(4):
                    if fill and q < 3:
                        fill(block_units + 5 if q == 0 else block_units)
                    elif fill:
                        fill.drain()
                    seen.need("norm_sq")
                    for t in range(4):
                        ins = pe.matmul(psC[:, 0:T], ones[:], sq[q % len(sq)][:, t * T:(t + 1) * T],
                                        start=(q == 0 and t == 0), stop=(q == 3 and t == 3))
                    ins.then_inc(sem("norm_sq_used"), 1)

            def heads_norm(per_head, buf, fill, fills):
                for _ in range(2):
                    seen.need("hn_sq")
                    if pe_n["hn"]:
                        pe.wait_ge(sem("hn_done"), pe_n["hn"])
                    pe_n["hn"] += 1
                    for t in range(4):
                        hd = t // per_head
                        ins = pe.matmul(psCD[:, hd * T:(hd + 1) * T], ones[:], buf[:, t * T:(t + 1) * T],
                                        start=(t % per_head == 0), stop=(t % per_head == per_head - 1))
                    ins.then_inc(sem("hn_sq_used"), 1)
                    fill(fills)

            def attention(which, n_heads, dt, q, k, v, fill, fills):
                h0 = HEAD0[which]

                def scores(h):
                    g = h0 + h
                    if g >= 2:
                        pe.wait_ge(sem("scores_read"), g - 1)
                    for tt in range(2):
                        for d in range(dt):
                            ins = pe.matmul(ps[:, 2 + g % 2, tt * T:(tt + 1) * T], q[:, h * dt + d, tt * P:(tt + 1) * P],
                                            k[:, h * dt + d, :], start=(d == 0), stop=(d == dt - 1))
                    ins.then_inc(sem("scores_done"), 1)

                scores(0)
                for h in range(n_heads):
                    g = h0 + h
                    if h + 1 < n_heads:
                        scores(h + 1)
                    fill(fills // 2)
                    pe.wait_ge(sem("p_ready"), g + 1)
                    if g:
                        pe.wait_ge(sem("pt_copied"), g)
                    for tt in range(2):
                        for kt in range(2):
                            ins = pe.transpose(psA[:, kt * T + tt * P:kt * T + (tt + 1) * P],
                                               att_s[g % 2][:, tt, kt * P:(kt + 1) * P], ident[:])
                    ins.then_inc(sem("p_turned"), 1)
                    fill(fills - fills // 2)
                    pe.wait_ge(sem("pt_copied"), g + 1)
                    if h:
                        pe.wait_ge(sem("y_t"), HEAD0[which] + h)
                    for d in range(dt):
                        for kt in range(2):
                            at = (h * dt + d) * P
                            ins = pe.matmul(psB[:, d * T:(d + 1) * T], v[:, kt, at:at + P], att_pt[:, kt, :],
                                            start=(kt == 0), stop=(kt == 1))
                    ins.then_inc(sem("pv_done"), 1)

            def pair(p, fill):

                def rows(hh):
                    return slice(64 * hh, 64 * hh + 64)

                def settle(ins):
                    ins.then_inc(sem("rows_done"), 1)
                    seen.need("rows_done")

                def products(hh, bank, left, right, name):
                    if hh:
                        seen.need("rows_done")
                    for c in range(2):
                        n = 2 * hh + c
                        ins = pe.matmul(bank[:, n * P:(n + 1) * P], left[rows(hh), c * P:(c + 1) * P],
                                        right[rows(hh), c * P:(c + 1) * P], start=True, stop=True)
                    ins.then_inc(sem(name if hh else "rows_done"), 1)

                cols = slice(p * P, (p + 1) * P)
                if p:
                    pe.wait_ge(sem("y_lo"), p)
                pe.matmul(psA[:, 0:T], w2a2[0:64, cols], lora_x[0:64, :], start=True, stop=True).then_inc(sem("rows_done"), 1)
                fill(0.5)
                seen.need("rows_done")
                pe.matmul(psA[:, T:2 * T], w2a2[64:128, cols], lora_x[64:128, :], start=True, stop=True).then_inc(sem("lora_z"), 1)
                fill(0.5)
                pe.wait_ge(sem("kk_sq"), p + 1)
                pe.matmul(psB[:, 0:T], blk[:], r_sq, start=True, stop=True).then_inc(sem("kk_sum"), 1)
                fill(3.5)
                pe.wait_ge(sem("ab_ready"), p + 1)
                for hh in range(2):
                    products(hh, psA, r_bt, r_at, "prod_abt")
                    products(hh, psD, r_at, r_bt, "prod_ab")
                pe.wait_ge(sem("kr_ready"), p + 1)
                products(0, psC, r_kt, r_at, "prod_ak")
                fill(0.5)
                products(1, psC, r_kt, r_at, "prod_ak")
                fill(0.5)
                pe.wait_ge(sem("abt_read"), p + 1)
                products(0, psA, r_bt, r_rt, "prod_rb")
                for l in range(1, LEVELS):
                    n = p * (LEVELS - 1) + l
                    if l == 1:
                        pe.wait_ge(sem("ab_read"), p + 1)
                    else:
                        pe.wait_ge(sem("x_ready"), n - 1)
                    for t in range(4):
                        ins = pe.matmul(packed(psB, l)[:, t], r_cm[:, t, :], one_of_pair(r_xt, l, 1)[:, t], start=True, stop=True)
                    ins.then_inc(sem("g_done"), 1)
                    if l == 1:
                        products(1, psA, r_bt, r_rt, "prod_rb")
                    if l == 2:
                        pe.wait_ge(sem("rk_read"), p + 1)
                        for t, src in enumerate((r_rkv[:, 2, 0:P], r_rkv[:, 2, P:T], r_bt[:, 0:P], r_kt[:, 0:P])):
                            ins = pe.transpose(psA[:, t * P:(t + 1) * P], src, ident[:])
                        ins.then_inc(sem("vbk_turned"), 1)
                    fill(0.5)
                    pe.wait_ge(sem("g_read"), n)
                    if l == 1:
                        pe.wait_ge(sem("ak_read"), p + 1)
                    for t in range(4):
                        ins = pe.matmul(packed(psC, l)[:, t], r_x[:, t, :], one_of_pair(r_g, l, 1)[:, t], start=True, stop=True)
                    if l < LEVELS - 1:
                        for t in range(4):
                            ins = pe.matmul(packed(psD, l)[:, t], r_g[:, t, :], one_of_pair(r_x, l, 0)[:, t], start=True, stop=True)
                    ins.then_inc(sem("xg_done"), 1)
                    if l == 1:
                        pe.wait_ge(sem("rb_read"), p + 1)
                        products(0, psA, r_kt, r_rt, "prod_rk")
                    fill(0.5)
                    if l == 1:
                        products(1, psA, r_kt, r_rt, "prod_rk")
                pe.wait_ge(sem("vbk_ready"), p + 1)
                for c in range(2):
                    vc = r_vbk[:, c, :]
                    if c:
                        pe.wait_ge(sem("s_read"), p + 1)
                    for hh in range(2):
                        o = psA[:, hh * 64:hh * 64 + 64]
                        if c:
                            settle(pe.matmul(o, r_at[rows(hh), P:T], r_s[rows(hh), :], start=True, stop=False))
                        ins = pe.matmul(o, r_ak[:, 2 * hh + c, :], vc[:, rows(hh)], start=not c, stop=True)
                    ins.then_inc(sem("w_done"), 1)
                    pe.wait_ge(sem("w_read"), 2 * p + c + 1)
                    if c == 0:
                        pe.wait_ge(sem("x_ready"), (p + 1) * (LEVELS - 1))
                    for hh in range(2):
                        ins = pe.matmul(psA[:, P + hh * 64:P + hh * 64 + 64], r_xt[:, 2 * hh + c, :],
                                        r_w[:, hh * 64:hh * 64 + 64], start=True, stop=True)
                    ins.then_inc(sem("u_done"), 1)
                    if c == 0:
                        fill(0.5)
                    pe.wait_ge(sem("u_read"), 2 * p + c + 1)
                    uc = r_u[:, c * P:(c + 1) * P]
                    if c == 0:
                        for hh in range(2):
                            o = psD[rows(hh), 0:64]
                            pe.matmul(o, r_vbk[:, 2, rows(hh)], uc[:, rows(hh)], start=True, stop=False)
                            ins = pe.matmul(o, r_vbk[:, 3, rows(hh)], vc[:, rows(hh)], start=False, stop=True)
                        ins.then_inc(sem("s_done"), 1)
                    for hh in range(2):
                        o = psB[rows(hh), c * P:(c + 1) * P]
                        pe.matmul(o, vc[:, rows(hh)], r_ark[:, 2 * hh + c, :], start=True, stop=False)
                        ins = pe.matmul(o, uc[:, rows(hh)], r_arb[:, 2 * hh + c, :], start=False, stop=not c)
                        if c:
                            ins = pe.matmul(o, r_s[rows(hh), :], r_rt[rows(hh), P:T], start=False, stop=True)
                ins.then_inc(sem("o_done"), 1)
                fill()
                pe.wait_ge(sem("o_read"), p + 1)
                pe.matmul(psC[:, 0:T], blk[:], r_o, start=True, stop=True).then_inc(sem("mean_done"), 1)
                pe.matmul(psD[:, 0:T], blk[:], r_rk, start=True, stop=True).then_inc(sem("bonus_done"), 1)
                fill()
                pe.wait_ge(sem("dev_sq"), p + 1)
                pe.matmul(psC[:, T:2 * T], blk[:], r_sq, start=True, stop=True).then_inc(sem("var_done"), 1)
                fill(2)

            pe.wait_ge(sem("ident_ready"), 1)
            for a in range(2):
                pe.wait_ge(sem(f"x_landed{a}"), 16)
            turn([[x_rows[:, a, t * P:(t + 1) * P] for t in (2 * g, 2 * g + 1) for a in range(2)] for g in range(8)])
            pe.wait_ge(sem("rows_landed"), 16 * N_ROW_DMAS)
            pe.transpose(psC[:, 0:n_rows1], rows1[0:n_rows1, :], ident[0:n_rows1, 0:n_rows1])
            pe.transpose(psC[:, P:P + n_rows2], rows2[0:n_rows2, :], ident[0:n_rows2, 0:n_rows2]).then_inc(sem("vec_turned"), 1)
            pe.wait_ge(sem("ones_ready"), 1)
            pe.wait_ge(sem("vec_ready"), 1)
            norm()
            fill = filler(unit, ["lora", "B0"])
            fill.drain()
            pe.wait_ge(sem("lora_ready"), 1)
            pe.wait_ge(sem("w2_landed"), 32)
            for p in range(KB):
                fill = fill_halves([f"B{p + 1}", f"A{p}"] if p + 1 < KB else [f"A{p}", "gate_b0"])
                pair(p, fill)
                fill.drain()
            values = lambda v: [[v[:, 4 * g + t, tt * P:(tt + 1) * P] for t in range(4)] for tt in range(2) for g in range(2)]
            fill = filler(unit, ["gate_b"])
            heads_norm(1, hn_sq, fill, 5)
            heads_norm(1, hn_sq, fill, 5)
            turn(values(a_vraw))
            fill.drain()
            fill = filler(unit, ["C"])
            pe.wait_ge(sem("hn_done"), 4)
            pe.wait_ge(sem("turn_copied"), pe_n["turn"])
            attention("a", 8, 1, a_q, a_k, att_v, fill, 4)
            fill.drain()
            run(pe, unit, "gate_a")
            pe.wait_ge(sem("mem_scaled"), 2)
            turn([[mem_rows[a][:, t * P:(t + 1) * P] for t in (2 * g, 2 * g + 1) for a in range(2)] for g in range(8)])
            run(pe, unit, "mem")
            fill = filler(unit, ["gate_c"])
            heads_norm(2, c_sq, fill, 2)
            heads_norm(2, c_sq, fill, 2)
            wait_evacuated(pe, phases["mem"][0] + 2)
            wait_evacuated(pe, phases["mem"][0] + 3)
            turn(values(c_vraw))
            fill(2)
            pe.wait_ge(sem("hn_done"), 8)
            pe.wait_ge(sem("turn_copied"), pe_n["turn"])
            attention("c", 4, 2, c_q, c_k, c_v, fill, 6)
            fill.drain()
            run(pe, unit, "up_c")
            norm(filler(unit, ["o"]))
            run(pe, unit, "Q")
            wait_evacuated(pe, phases["L"][0] - 1)
            wait_evacuated(pe, phases["L"][0] - 2)
            turn(values(q_vraw))
            pe.wait_ge(sem("turn_copied"), pe_n["turn"])
            fill = filler(unit, ["L", "down"])
            attention("q", 8, 1, q_q, q_k, att_v, fill, 6)
            fill.drain()
            pe.wait_ge(sem("y_lo"), KB + 20)
            run(pe, unit, "gate_1")
            turn(values(l_vraw))
            fill = filler(unit, [f"V{p}" for p in range(KB)])
            pe.wait_ge(sem("up_landed"), 16)
            pe.wait_ge(sem("turn_copied"), pe_n["turn"])
            for h in range(4):
                ins = pe.matmul(ps[:, h // 2, h % 2 * T:(h % 2 + 1) * T], l_up[0:16, h * P:(h + 1) * P], l_down[0:16, :], start=True, stop=True)
            ins.then_inc(sem("gla_z"), 1)
            fill(4)
            for h in range(4):
                pe.wait_ge(sem("gla_in"), h + 1)
                for tt in range(2):
                    pe.matmul(psB[:, tt * P:(tt + 1) * P], l_kin[:, tt * P:(tt + 1) * P], l_qin[:, tt * P:(tt + 1) * P],
                              start=True, stop=True)
                for tt in range(2):
                    ins = pe.transpose(psB[:, T + tt * P:T + (tt + 1) * P], l_kin[:, tt * P:(tt + 1) * P], ident[:])
                ins.then_inc(sem("gla_a"), 1)
                fill(1)
                if h:
                    pe.wait_ge(sem("gla_y"), h)
                pe.wait_ge(sem("gla_a_read"), h + 1)
                for c in range(3):
                    half = slice(64 * (c % 2), 64 * (c % 2) + 64)
                    if c == 2:
                        pe.wait_ge(sem("gla_s"), 3 * h + 1)
                    pe.matmul((psA if c % 2 == 0 else psD)[:, T:2 * T], l_kt[half, c // 2, :], l_v[half, c // 2, h * T:(h + 1) * T],
                              start=True, stop=True).then_inc(sem("gla_kv"), 1)
                for e in range(2):
                    for tt in range(2):
                        at = h * T + e * P
                        pe.matmul(psC[:, e * T + tt * P:e * T + (tt + 1) * P], l_v[:, tt, at:at + P], l_at[:, tt, :],
                                  start=(e == 0 and tt == 0), stop=(tt == 0), skip_group_check=True)
                fill(4)
                pe.wait_ge(sem("gla_s"), 3 * h + 3)
                for e in range(2):
                    for c in range(1, 4):
                        ins = pe.matmul(psC[:, e * T + 64 * c:e * T + 64 * c + 64], l_s[c - 1][:, e * P:(e + 1) * P],
                                        l_qin[:, 64 * c:64 * c + 64], start=False, stop=True, skip_group_check=True)
                ins.then_inc(sem("gla_o"), 1)
                fill(5)
                pe.wait_ge(sem("gla_sq"), h + 1)
                for e in range(2):
                    ins = pe.matmul(psD[:, 0:T], ones[:], l_sq[:, e, :], start=(e == 0), stop=(e == 1))
                ins.then_inc(sem("gla_ss"), 1)
                fill(5)
            fill.drain()
            pe.wait_ge(sem("y_lo"), KB + 24)
            run(pe, unit, "gate_2")
            run(pe, unit, "gate_3")
            norm(filler(unit, ["o2"]))
            run(pe, unit, "ffn")
            norm(filler(unit, ["ffn_down"]), KF // 2, last_sq)
            pe.wait_ge(sem("norm_t"), 16)
            turn([[x_t[:, 4 * g + t, a * P:(a + 1) * P] for t in range(4)] for a in range(2) for g in range(4)])


def kernel(**inputs):
    from concourse import bacc
    from concourse.bass_utils import run_bass_kernel_spmd

    nc = bacc.Bacc("TRN2", target_bir_lowering=False, num_devices=1)
    arrays, dram = {}, {}
    for name, a in inputs.items():
        a = np.ascontiguousarray(a)
        arrays[f"in_{name}"] = a
        dram[name] = nc.dram_tensor(f"in_{name}", a.shape, mybir.dt.from_np(a.dtype), kind="ExternalInput").ap()
    out = nc.dram_tensor("out_x", (1, T, D), F32, kind="ExternalOutput").ap()
    build(nc, dram, out)
    r = run_bass_kernel_spmd(nc, [arrays], core_ids=[0])
    return r.results[0]["out_x"]
```
